# Optimizing a Trainium2 kernel written in Bass

```python
import jax, jax.numpy as jnp
from jax import lax
import numpy as np

D_MODEL = 1024
BATCH = 1
SEQ = 256
DEPTH = 1

HEAD_DIM = 64
MOBA_HEADS = 8
NSA_HEADS = 8
NSA_KV_HEADS = 2
NSA_GROUP = NSA_HEADS // NSA_KV_HEADS
MIX_WIDTH = (MOBA_HEADS + NSA_HEADS) * HEAD_DIM
MOBA_BLOCK = 256
MOBA_TOPK = 3
NSA_CMP_LEN = 32
NSA_CMP_STRIDE = 16
NSA_SLC_BLOCK = 64
NSA_SLC_TOPN = 16
NSA_WINDOW = 512
NSA_BRANCHES = 3
N_EXPERTS = 32
TOP_K = 4
D_FF = D_MODEL
SWIGLU_LIMIT = 7.0
SWIGLU_ALPHA = 1.702
MOE_ROW_BLOCK = 256
Q_BLOCK = 64
RMS_EPS = 1e-5
NEG_BIG = -1e30
NSA_GATE_COLS = NSA_BRANCHES * NSA_HEADS
IN_COLS = 3 * MOBA_HEADS * HEAD_DIM + NSA_HEADS * HEAD_DIM + 2 * NSA_BRANCHES * NSA_KV_HEADS * HEAD_DIM + NSA_GATE_COLS

kernel_name = 'hybrid_moba_nsa_moe_alibi'

def rmsnorm(x, g):
    xf = x.astype(jnp.float32)
    y = xf * lax.rsqrt(jnp.mean(xf * xf, axis=-1, keepdims=True) + RMS_EPS)
    return (y * g.astype(jnp.float32)).astype(x.dtype)

def masked_softmax(logits, mask):
    z = jnp.where(mask, logits, NEG_BIG)
    z = z - jnp.max(z, axis=-1, keepdims=True)
    p = jnp.where(mask, jnp.exp(z), 0.0)
    return p / jnp.maximum(jnp.sum(p, axis=-1, keepdims=True), 1e-30)

def alibi_slopes():
    n = MOBA_HEADS + NSA_HEADS
    s = jnp.exp2(-8.0 * jnp.arange(1, n + 1, dtype=jnp.float32) / n)
    return s[0::2], s[1::2]

def moba_attention(q, k, v, slopes):
    B, S, H, hd = q.shape
    nb = -(-S // MOBA_BLOCK)
    pad = nb * MOBA_BLOCK - S
    padw = ((0, 0), (0, pad), (0, 0), (0, 0))
    kb = jnp.pad(k, padw).reshape(B, nb, MOBA_BLOCK, H, hd).transpose(0, 3, 1, 2, 4)
    vb = jnp.pad(v, padw).reshape(B, nb, MOBA_BLOCK, H, hd).transpose(0, 3, 1, 2, 4)
    kmean = jnp.mean(kb.astype(jnp.float32), axis=3)
    qh = q.transpose(0, 2, 1, 3) * (hd ** -0.5)
    topk = min(MOBA_TOPK, nb)
    nsel = topk * MOBA_BLOCK
    bi = jnp.arange(B)[:, None, None, None]
    hi = jnp.arange(H)[None, :, None, None]
    sl = slopes[None, :, None, None]
    offs = jnp.arange(MOBA_BLOCK)

    def chunk(c):
        t0 = c * Q_BLOCK
        qc = lax.dynamic_slice_in_dim(qh, t0, Q_BLOCK, axis=2)
        t = t0 + jnp.arange(Q_BLOCK)
        cur = t // MOBA_BLOCK
        gate = jnp.einsum('bhcd,bhnd->bhcn', qc.astype(jnp.float32), kmean)
        past = jnp.arange(nb)[None, :] < cur[:, None]
        _, idx = lax.top_k(jnp.where(past, gate, -jnp.inf), topk)
        ksel = kb[bi, hi, idx]
        vsel = vb[bi, hi, idx]
        pos_sel = idx[..., None] * MOBA_BLOCK + offs
        dist_sel = (t[None, None, :, None, None] - pos_sel).astype(jnp.float32)
        s_sel = jnp.einsum('bhcd,bhcnjd->bhcnj', qc, ksel, preferred_element_type=jnp.float32) - sl[..., None] * dist_sel
        mask_sel = jnp.broadcast_to((jnp.arange(topk)[None, :] < cur[:, None])[None, None, :, :, None], s_sel.shape)
        cb = t0 // MOBA_BLOCK
        kown = lax.dynamic_index_in_dim(kb, cb, axis=2, keepdims=False)
        vown = lax.dynamic_index_in_dim(vb, cb, axis=2, keepdims=False)
        pos_own = cb * MOBA_BLOCK + offs
        dist_own = (t[:, None] - pos_own[None, :]).astype(jnp.float32)
        s_own = jnp.einsum('bhcd,bhjd->bhcj', qc, kown, preferred_element_type=jnp.float32) - sl * dist_own
        mask_own = jnp.broadcast_to((dist_own >= 0)[None, None], s_own.shape)
        logits = jnp.concatenate([s_sel.reshape(B, H, Q_BLOCK, nsel), s_own], axis=-1)
        mask = jnp.concatenate([mask_sel.reshape(B, H, Q_BLOCK, nsel), mask_own], axis=-1)
        p = masked_softmax(logits, mask).astype(v.dtype)
        out = jnp.einsum('bhcm,bhcmd->bhcd', p[..., :nsel], vsel.reshape(B, H, Q_BLOCK, nsel, hd))
        return out + jnp.einsum('bhcj,bhjd->bhcd', p[..., nsel:], vown)

    outs = lax.map(chunk, jnp.arange(S // Q_BLOCK))
    return outs.transpose(1, 0, 3, 2, 4).reshape(B, S, H * hd)

def compress_blocks(kv, pe, w1, w2):
    B, S, G, hd = kv.shape
    n_cmp = (S - NSA_CMP_LEN) // NSA_CMP_STRIDE + 1
    idx = jnp.arange(n_cmp)[:, None] * NSA_CMP_STRIDE + jnp.arange(NSA_CMP_LEN)[None, :]
    blk = kv[:, idx] + pe[None, None, :, None, :]
    flat = blk.transpose(0, 1, 3, 2, 4).reshape(B, n_cmp, G, NSA_CMP_LEN * hd)
    return jax.nn.gelu(flat @ w1) @ w2

def nsa_attention(q, kc, vc, ks, vs, kw, vw, gate_logits, pe_k, pe_v, w1_k, w2_k, w1_v, w2_v, slopes):
    B, S, Hq, hd = q.shape
    G, Hg = NSA_KV_HEADS, NSA_GROUP
    dt = q.dtype
    n_cmp = (S - NSA_CMP_LEN) // NSA_CMP_STRIDE + 1
    n_slc = S // NSA_SLC_BLOCK
    topn = min(NSA_SLC_TOPN, n_slc)
    W = NSA_WINDOW
    kcmp = compress_blocks(kc, pe_k, w1_k, w2_k)
    vcmp = compress_blocks(vc, pe_v, w1_v, w2_v)
    cmp_pos = jnp.arange(n_cmp) * NSA_CMP_STRIDE + NSA_CMP_LEN - 1
    cu, su = NSA_CMP_LEN // NSA_CMP_STRIDE, NSA_SLC_BLOCK // NSA_CMP_STRIDE
    ii = jnp.arange(n_cmp)[:, None]
    jj = jnp.arange(n_slc)[None, :]
    overlap = jnp.clip(jnp.minimum(ii + cu, (jj + 1) * su) - jnp.maximum(ii, jj * su), 0, None).astype(jnp.float32)
    qh = q.reshape(B, S, G, Hg, hd).transpose(0, 2, 3, 1, 4) * (hd ** -0.5)
    ksb = ks.reshape(B, n_slc, NSA_SLC_BLOCK, G, hd).transpose(0, 3, 1, 2, 4)
    vsb = vs.reshape(B, n_slc, NSA_SLC_BLOCK, G, hd).transpose(0, 3, 1, 2, 4)
    padw = ((0, 0), (W, 0), (0, 0), (0, 0))
    kwp = jnp.pad(kw, padw).transpose(0, 2, 1, 3)
    vwp = jnp.pad(vw, padw).transpose(0, 2, 1, 3)
    gates = jax.nn.sigmoid(gate_logits.astype(jnp.float32)).reshape(B, S, G, Hg, NSA_BRANCHES).transpose(0, 2, 3, 1, 4)
    sl = slopes.reshape(G, Hg)[None, :, :, None, None]
    bi = jnp.arange(B)[:, None, None, None]
    gi = jnp.arange(G)[None, :, None, None]
    soffs = jnp.arange(NSA_SLC_BLOCK)
    nwin = Q_BLOCK + W - 1
    nsel = topn * NSA_SLC_BLOCK

    def chunk(c):
        t0 = c * Q_BLOCK
        qc = lax.dynamic_slice_in_dim(qh, t0, Q_BLOCK, axis=3)
        t = t0 + jnp.arange(Q_BLOCK)
        dist_c = (t[:, None] - cmp_pos[None, :]).astype(jnp.float32)
        s_c = jnp.einsum('bghcd,bngd->bghcn', qc, kcmp, preferred_element_type=jnp.float32)
        p_c = masked_softmax(s_c - sl * dist_c, dist_c >= 0)
        o_c = jnp.einsum('bghcn,bngd->bghcd', p_c.astype(dt), vcmp)
        imp = jnp.einsum('bghcn,nj->bgcj', p_c, overlap)
        cur = t // NSA_SLC_BLOCK
        jr = jnp.arange(n_slc)[None, :]
        forced = (jr == 0) | (jr == cur[:, None]) | (jr == cur[:, None] - 1)
        allowed = jr <= cur[:, None]
        score = jnp.where(allowed, jnp.where(forced, jnp.inf, imp), -jnp.inf)
        _, sidx = lax.top_k(score, topn)
        ksel = ksb[bi, gi, sidx]
        vsel = vsb[bi, gi, sidx]
        pos_s = sidx[..., None] * NSA_SLC_BLOCK + soffs
        dist_s = (t[None, None, :, None, None] - pos_s).astype(jnp.float32)[:, :, None]
        s_s = jnp.einsum('bghcd,bgcnjd->bghcnj', qc, ksel, preferred_element_type=jnp.float32) - sl[..., None] * dist_s
        p_s = masked_softmax(s_s.reshape(B, G, Hg, Q_BLOCK, nsel), (dist_s >= 0).reshape(B, G, 1, Q_BLOCK, nsel))
        o_s = jnp.einsum('bghcm,bgcmd->bghcd', p_s.astype(dt), vsel.reshape(B, G, Q_BLOCK, nsel, hd))
        kwin = lax.dynamic_slice_in_dim(kwp, t0 + 1, nwin, axis=2)
        vwin = lax.dynamic_slice_in_dim(vwp, t0 + 1, nwin, axis=2)
        pos_w = t0 - W + 1 + jnp.arange(nwin)
        dist_w = t[:, None] - pos_w[None, :]
        mask_w = (dist_w >= 0) & (dist_w < W) & (pos_w[None, :] >= 0)
        s_w = jnp.einsum('bghcd,bgjd->bghcj', qc, kwin, preferred_element_type=jnp.float32)
        p_w = masked_softmax(s_w - sl * dist_w.astype(jnp.float32), mask_w)
        o_w = jnp.einsum('bghcj,bgjd->bghcd', p_w.astype(dt), vwin)
        g = lax.dynamic_slice_in_dim(gates, t0, Q_BLOCK, axis=3).astype(dt)
        return g[..., 0:1] * o_c + g[..., 1:2] * o_s + g[..., 2:3] * o_w

    outs = lax.map(chunk, jnp.arange(S // Q_BLOCK))
    return outs.transpose(1, 0, 4, 2, 3, 5).reshape(B, S, Hq * hd)

def clamped_swiglu(h):
    g = jnp.minimum(h[..., 0::2], SWIGLU_LIMIT)
    u = jnp.clip(h[..., 1::2], -SWIGLU_LIMIT, SWIGLU_LIMIT)
    return g * jax.nn.sigmoid(SWIGLU_ALPHA * g) * (u + 1.0)

def moe_ffn(h, w_router, b_router, w_up, b_up, w_down, b_down):
    B, S, D = h.shape
    N = B * S
    NK = N * TOP_K
    ht = h.reshape(N, D)
    logits = (ht @ w_router + b_router).astype(jnp.float32)
    top_val, top_idx = lax.top_k(logits, TOP_K)
    wts = jax.nn.softmax(top_val, axis=-1)
    flat_e = top_idx.reshape(NK)
    flat_tok = jnp.repeat(jnp.arange(N, dtype=jnp.int32), TOP_K)
    order = jnp.argsort(flat_e, stable=True)
    se, stok, sw = flat_e[order], flat_tok[order], wts.reshape(NK)[order]
    counts = jnp.bincount(flat_e, length=N_EXPERTS)
    starts = jnp.cumsum(counts) - counts
    padded = (counts + MOE_ROW_BLOCK - 1) // MOE_ROW_BLOCK * MOE_ROW_BLOCK
    pends = jnp.cumsum(padded)
    pstarts = pends - padded
    dest = pstarts[se] + jnp.arange(NK) - starts[se]
    n_blk = (NK + N_EXPERTS * MOE_ROW_BLOCK + MOE_ROW_BLOCK - 1) // MOE_ROW_BLOCK
    P = n_blk * MOE_ROW_BLOCK
    row_tok = jnp.full((P,), N, jnp.int32).at[dest].set(stok)
    xrows = jnp.concatenate([ht, jnp.zeros((1, D), ht.dtype)], axis=0)[row_tok].reshape(n_blk, MOE_ROW_BLOCK, D)
    blk_e = jnp.minimum(jnp.searchsorted(pends, jnp.arange(n_blk) * MOE_ROW_BLOCK, side='right'), N_EXPERTS - 1)

    def expert_block(args):
        xb, e = args
        a = clamped_swiglu(xb @ w_up[e] + b_up[e])
        return a @ w_down[e] + b_down[e]

    yrows = lax.map(expert_block, (xrows, blk_e)).reshape(P, D)
    contrib = yrows[dest] * sw[:, None].astype(yrows.dtype)
    return jax.ops.segment_sum(contrib, stok, num_segments=N).reshape(B, S, D)

def setup_inputs(seed: int = 0) -> dict:
    key = jax.random.key(seed)
    k = jax.random.split(key, 20)
    hd, L = HEAD_DIM, NSA_CMP_LEN

    def nrm(kk, shape, scale):
        return jax.random.normal(kk, shape, jnp.float32) * scale

    return {
        'x': nrm(k[0], (BATCH, SEQ, D_MODEL), 1.0),
        'attn_norm_g': 1.0 + nrm(k[1], (DEPTH, D_MODEL), 0.02),
        'w_in': nrm(k[2], (DEPTH, D_MODEL, IN_COLS), D_MODEL ** -0.5),
        'cmp_pe_k': nrm(k[3], (DEPTH, L, hd), 0.1),
        'cmp_pe_v': nrm(k[4], (DEPTH, L, hd), 0.1),
        'cmp_w1_k': nrm(k[5], (DEPTH, L * hd, hd), (L * hd) ** -0.5),
        'cmp_w2_k': nrm(k[6], (DEPTH, hd, hd), hd ** -0.5),
        'cmp_w1_v': nrm(k[7], (DEPTH, L * hd, hd), (L * hd) ** -0.5),
        'cmp_w2_v': nrm(k[8], (DEPTH, hd, hd), hd ** -0.5),
        'w_out': nrm(k[9], (DEPTH, MIX_WIDTH, D_MODEL), MIX_WIDTH ** -0.5),
        'ffn_norm_g': 1.0 + nrm(k[10], (DEPTH, D_MODEL), 0.02),
        'w_router': nrm(k[11], (DEPTH, D_MODEL, N_EXPERTS), D_MODEL ** -0.5),
        'b_router': nrm(k[12], (DEPTH, N_EXPERTS), 0.01),
        'w_up': nrm(k[13], (DEPTH, N_EXPERTS, D_MODEL, 2 * D_FF), D_MODEL ** -0.5),
        'b_up': nrm(k[14], (DEPTH, N_EXPERTS, 2 * D_FF), 0.01),
        'w_down': nrm(k[15], (DEPTH, N_EXPERTS, D_FF, D_MODEL), D_FF ** -0.5),
        'b_down': nrm(k[16], (DEPTH, N_EXPERTS, D_MODEL), 0.01),
        'final_norm_g': 1.0 + nrm(k[17], (D_MODEL,), 0.02),
    }

def reference(x, attn_norm_g, w_in, cmp_pe_k, cmp_pe_v, cmp_w1_k, cmp_w2_k, cmp_w1_v, cmp_w2_v, w_out, ffn_norm_g, w_router, b_router, w_up, b_up, w_down, b_down, final_norm_g):
    B, S, _ = x.shape
    moba_sl, nsa_sl = alibi_slopes()
    sizes = [MOBA_HEADS * HEAD_DIM] * 3 + [NSA_HEADS * HEAD_DIM] + [NSA_KV_HEADS * HEAD_DIM] * (2 * NSA_BRANCHES) + [NSA_GATE_COLS]
    cuts = [int(c) for c in np.cumsum(sizes)[:-1]]

    def heads(t, n):
        return t.reshape(B, S, n, HEAD_DIM)

    for l in range(DEPTH):
        xn = rmsnorm(x, attn_norm_g[l])
        mq, mk, mv, nq, kc, vc, ks, vs, kw, vw, ng = jnp.split(xn @ w_in[l], cuts, axis=-1)
        o_moba = moba_attention(heads(mq, MOBA_HEADS), heads(mk, MOBA_HEADS), heads(mv, MOBA_HEADS), moba_sl)
        o_nsa = nsa_attention(heads(nq, NSA_HEADS), heads(kc, NSA_KV_HEADS), heads(vc, NSA_KV_HEADS),
                              heads(ks, NSA_KV_HEADS), heads(vs, NSA_KV_HEADS), heads(kw, NSA_KV_HEADS),
                              heads(vw, NSA_KV_HEADS), ng, cmp_pe_k[l], cmp_pe_v[l], cmp_w1_k[l],
                              cmp_w2_k[l], cmp_w1_v[l], cmp_w2_v[l], nsa_sl)
        x = x + jnp.concatenate([o_moba, o_nsa], axis=-1) @ w_out[l]
        x = x + moe_ffn(rmsnorm(x, ffn_norm_g[l]), w_router[l], b_router[l], w_up[l], b_up[l], w_down[l], b_down[l])
    return rmsnorm(x, final_norm_g)


_drawn_inputs = setup_inputs


def setup_inputs(seed=0):
    import zlib

    import numpy as np

    out = dict(_drawn_inputs(seed))
    spreads = {}
    factors = {'cmp_pe_k': 3.153, 'b_up': 8.0, 'b_down': 8.0, 'final_norm_g': 2.872}
    for name, (base, spread) in spreads.items():
        noise = np.random.default_rng([zlib.crc32(name.encode()), seed]).standard_normal(out[name].shape)
        drawn = base * np.exp(spread * noise) if base else spread * noise
        out[name] = __import__('jax').numpy.asarray(drawn.astype(out[name].dtype))
    for name, factor in factors.items():
        out[name] = (out[name] * factor).astype(out[name].dtype)
    return out
```

```python
from contextlib import ExitStack

import concourse.bass as bass
from concourse import mybir

P = 128
ALU = mybir.AluOpType
ACT = mybir.ActivationFunctionType
AX = mybir.AxisListType
F32 = mybir.dt.float32
I32 = mybir.dt.int32
U32 = mybir.dt.uint32
ds = bass.ds

TOK = 64
CAP = 64
BIG = 1e33
EPS = 1e-5


def hybrid_layer(nc, x, attn_norm_g, w_in, cmp_pe_k, cmp_pe_v, cmp_w1_k, cmp_w2_k, cmp_w1_v, cmp_w2_v, w_out,
                 ffn_norm_g, w_router, b_router, w_up, b_up, w_down, b_down, final_norm_g, out):
    _, S, D = x.shape
    E = w_router.shape[2]
    F = w_down.shape[2]
    HD = 64
    H = 8
    G = 2
    HG = H // G
    NT = S // P
    KD = D // P
    NC = (S - 32) // 16 + 1
    CMP_L = 32
    LP = CMP_L // 2
    TOPK = 4
    IN = w_in.shape[2]
    assert NT == 2 and KD == 8 and D == 1024 and F == 1024 and E == 32 and IN == 2840

    moba_slope = [2.0 ** (-8.0 * (2 * h + 1) / 16) for h in range(H)]
    nsa_slope = [2.0 ** (-8.0 * (2 * h + 2) / 16) for h in range(H)]
    nsa_order = [g * HG + j for j in range(HG) for g in range(G)]

    MORE = -(-S // CAP) - 1
    NOV = S * TOPK // (CAP + 1)

    CHUNK = 512
    chunk_width = [min(CHUNK, IN - c * CHUNK) for c in range(-(-IN // CHUNK))]
    UNITS = 12
    UNIT = 2048
    UP_UNITS = 8
    DOWN_UNITS = 4

    slots = [("moba", h) for h in range(H)] + [("slc", h) for h in nsa_order] + [("win", h) for h in nsa_order]
    NSLOT = len(slots)
    T_LAG, PV_LAG = 2, 3
    ZB = 4
    pre_jobs = ["mq0", "mk0"]
    slot_jobs = ["mv0", "mv1", "mq1", "mk1", "nq0", "kwvw", "vw1", "ksvs", "kcvc", "nq1"]
    jobs = pre_jobs + slot_jobs
    job_at = {n: i for i, n in enumerate(jobs)}
    last_job_of_chunk = {0: "mq1", 1: "mk1", 2: "mv1", 3: "nq1", 4: "kcvc", 5: "vw1"}
    CM1_SLOT, CM2_SLOT, CS_SLOT, CT_SLOT = 11, 13, 15, 19

    ctx = ExitStack()
    with ctx:
        def sb(name, shape, dt=F32):
            return ctx.enter_context(nc.sbuf_tensor(name, shape, dt))

        def sem(name):
            return ctx.enter_context(nc.semaphore(name))

        ps = ctx.enter_context(nc.psum_tensor("ps", [P, 8, 512], F32))

        ring = sb("ring", [P, UNITS, UNIT])
        wout = sb("wout", [P, KD, D])
        xt = sb("xt", [P, NT, D])
        xs = sb("xs", [P, NT, D])
        xT = sb("xT", [P, KD, S])
        ident = sb("ident", [P, P])
        upper = sb("upper", [P, P])
        ones = sb("ones", [P, P])
        prm = sb("prm", [48, P])
        prmT = sb("prmT", [P, 48])
        w2k = sb("w2k", [HD, HD])
        w2v = sb("w2v", [HD, HD])
        wr = sb("wr", [P, KD, E])
        br = sb("br", [P, E])
        sq_sum = sb("sq_sum", [P, 6])
        ms = sb("ms", [P, 6])
        root = sb("root", [P, 6])
        rstd = sb("rstd", [P, 6])
        w1k = wout[:, 0, :].rearrange("p (c j) -> p c j", j=HD)
        w1v = wout[:, 1, :].rearrange("p (c j) -> p c j", j=HD)
        gaT = prmT[:, 0:KD]
        gfT = prmT[:, KD:2 * KD]
        peT = [prmT[:, 16:32], prmT[:, 32:48]]

        WORK = 13280
        work = sb("work", [P, WORK])
        at = [0]

        def carve(n, *dims):
            a = work[:, at[0]:at[0] + n]
            at[0] += n
            assert at[0] <= WORK
            if len(dims) == 2:
                return a.rearrange("p (a b) -> p a b", a=dims[0])
            if len(dims) == 3:
                return a.rearrange("p (a b c) -> p a b c", a=dims[0], b=dims[1])
            return a

        mqT = carve(1024, 4, 256)
        mkT = carve(1024, 4, 256)
        nqT = carve(1024, 4, 256)
        ksT = carve(256)
        kwT = carve(256)
        mv = carve(1024, 2, 512)
        vs = carve(256, 2, 128)
        vw = carve(256, 2, 128)
        gates = carve(48, 2, 24)
        gtmp = carve(48, 2, 24)
        tabs = carve(8 * 256, 8, 256)
        dist = carve(256)
        z = carve(ZB * 384, ZB, 384)
        pT = carve(2 * 384, 2, 384)
        zmin = carve(2 * ZB, ZB, 2)
        zsum = carve(2 * ZB, ZB, 2)
        zrec = carve(2 * ZB, ZB, 2)
        R = [carve(2 * LP * 15, 2, LP, 15) for _ in range(2)]
        hx = carve(64)
        hsq = carve(64)
        ht = carve(64)
        hTk = carve(32)
        hTv = carve(2 * 128, 2, 4, 32)
        kcT = carve(16)
        vc = carve(2 * 256, 2, 256)
        cdist = carve(32, 2, 16)
        cmask = carve(32, 2, 16)
        ctab = carve(2 * 8 * 16, 2, 8, 16)
        cz = carve(2 * 8 * 32, 2, 8, 32)
        cmin = carve(16, 2, 8)
        csum = carve(16, 2, 8)
        crec = carve(16, 2, 8)
        pcT = carve(4 * 128, 4, 128)
        at[0] = 0
        iota_e = carve(32)
        iota_t = carve(128)
        lg = carve(64, 2, 32)
        top = carve(16, 2, 8)
        topi = carve(16, 2, 8).bitcast(U32)
        topf = carve(8, 2, 4)
        hot = carve(8 * 32, 2, 4, 32)
        hotw = carve(8 * 32, 2, 4, 32)
        tdiff = carve(8, 2, 4)
        texp = carve(8, 2, 4)
        tsum = carve(2)
        trec = carve(2)
        tw = carve(8, 2, 4)
        M = carve(64, 2, 32)
        posp = carve(66, 2, 33)
        Wt = carve(66, 2, 33)
        WT = carve(256)
        bd = carve(1024)
        gfin = carve(1024)
        brow = carve(2048)
        pcol = carve(2)
        pm = carve(128, 2, 64)
        pw = carve(256, 2, 128)
        xg = carve(512)
        xgT = carve(512, 8, 64)
        t1 = carve(512, 2, 256)
        t2 = carve(512, 2, 256)
        t3 = carve(512, 2, 256)
        av = carve(512, 2, 256)
        aT = carve(512, 4, 128)
        yv = carve(512)
        cT = carve(256, 2, 128)
        cnt = carve(1)
        ecol = carve(1)
        more_k = carve(MORE)
        flag = carve(MORE)
        nflag = carve(1)
        rank = carve(MORE)
        iota_o = carve(NOV)
        Rsel = carve(MORE * NOV, MORE, NOV)
        Rk = carve(NOV)
        Re = carve(NOV)
        Rb = carve(NOV)
        ovt = carve(2 * NOV + 1)
        ovi = carve(2 * NOV + 1).bitcast(I32)

        PJ = [0, 1]
        SB = [2, 3]
        TB = [4, 5]
        OB = [6, 7]
        XG, XTB = 0, 1
        UP = ps[:, 2:4, :]
        OUT = [[4, 5], [6, 7]]

        x_in = [sem(f"x_in{n}") for n in range(NT)]
        unit_in = [sem(f"unit_in{u}") for u in range(UNITS)]
        prm_in = sem("prm_in")
        cmpw_in = sem("cmpw_in")
        wout_in = [sem(f"wout_in{n}") for n in range(4)]
        router_in = sem("router_in")
        late_in = sem("late_in")
        brow_in = sem("brow_in")
        out_sent = sem("out_sent")
        ident_ready = sem("ident_ready")
        const_ready = sem("const_ready")
        pool_chain = sem("pool_chain")
        dist_ready = sem("dist_ready")
        tab_ready = sem("tab_ready")
        ctab_ready = sem("ctab_ready")
        iotas_ready = sem("iotas_ready")
        gfin_ready = sem("gfin_ready")
        prmT_ps = sem("prmT_ps")
        prmT_ready = sem("prmT_ready")
        squared = sem("squared")
        rooted = sem("rooted")
        dve_chain = sem("dve_chain")
        ms_ready = sem("ms_ready")
        xs_ready = sem("xs_ready")
        xT_ps = sem("xT_ps")
        xT_ready = sem("xT_ready")
        job_done = sem("job_done")
        job_read = sem("job_read")
        r_ready = sem("r_ready")
        gate_exp = sem("gate_exp")
        gates_ready = sem("gates_ready")
        s_done = sem("s_done")
        z_done = sem("z_done")
        exp_done = sem("exp_done")
        p_scaled = sem("p_scaled")
        pT_done = sem("pT_done")
        pT_read = sem("pT_read")
        pv_done = sem("pv_done")
        o_read = sem("o_read")
        cm1_done = sem("cm1_done")
        gelu_t = sem("gelu_t")
        gelu_exp = sem("gelu_exp")
        gelu_done = sem("gelu_done")
        cm2_done = sem("cm2_done")
        cm2_read = sem("cm2_read")
        cs_done = sem("cs_done")
        cz_ready = sem("cz_ready")
        cexp_done = sem("cexp_done")
        cp_ready = sem("cp_ready")
        cpT_done = sem("cpT_done")
        cpT_read = sem("cpT_read")
        proj_done = sem("proj_done")
        x2_ready = sem("x2_ready")
        logits_done = sem("logits_done")
        td_ready = sem("td_ready")
        te_ready = sem("te_ready")
        m_ready = sem("m_ready")
        pos_done = sem("pos_done")
        w_ready = sem("w_ready")
        wT_done = sem("wT_done")
        wT_read = sem("wT_read")
        nflag_ready = sem("nflag_ready")
        rank_done = sem("rank_done")
        rsel_ready = sem("rsel_ready")
        ovt_done = sem("ovt_done")
        ovi_ready = sem("ovi_ready")
        pcol_ready = sem("pcol_ready")
        pm_ready = sem("pm_ready")
        pw_ready = sem("pw_ready")
        xg_done = sem("xg_done")
        xg_read = sem("xg_read")
        xgT_done = sem("xgT_done")
        xgT_read = sem("xgT_read")
        bias_used = sem("bias_used")
        up_used = sem("up_used")
        swi = sem("swi")
        sig_done = sem("sig_done")
        a_ready = sem("a_ready")
        aT_done = sem("aT_done")
        aT_read = sem("aT_read")
        down_used = sem("down_used")
        y_read = sem("y_read")
        cT_done = sem("cT_done")
        cT_read = sem("cT_read")
        comb_done = sem("comb_done")
        fin_ready = sem("fin_ready")

        x_v = x.rearrange("o (n p) d -> (o n) p d", p=P)
        out_v = out.rearrange("o (n p) d -> (o n) p d", p=P)
        win_v = w_in.rearrange("o (k p) n -> p (o k) n", p=P)
        wout_v = w_out.rearrange("o (k p) n -> p (o k) n", p=P)
        up_v = w_up.rearrange("o e (k p) f -> (o e) k p f", p=P)
        down_v = w_down.rearrange("o e (u j p) d -> (o e) u p j d", j=2, p=P)
        bup_v = b_up.rearrange("o e f -> (o e) f")

        def win_unit(c, k):
            w = chunk_width[c]
            return ring[:, 2 * c + k // 4, (k % 4) * w:(k % 4) * w + w]

        def cmp_tokens(src, parity):
            return bass.AP(tensor=src.tensor, offset=src.offset + parity, ap=[list(src.ap[0]), [2, LP], [16, NC]])

        def head_of(slot):
            kind, h = slots[slot]
            if kind == "moba":
                b = (h % 2) * HD
                return (mqT[b:b + HD, h // 2, :], mkT[b:b + HD, h // 2, :],
                        lambda t: mv[:, t, h * HD:(h + 1) * HD], h * HD)
            g, j = h // HG, h % HG
            b = g * HD
            kT, v = (ksT, vs) if kind == "slc" else (kwT, vw)
            return nqT[b:b + HD, j, :], kT[b:b + HD, :], lambda t: v[:, t, b:b + HD], h * HD

        def score_jobs(slot):
            kind, h = slots[slot]
            if kind == "moba":
                need = ["mq0", "mk0"] if h < 4 else ["mq1", "mk1"]
            else:
                need = ["nq0" if h % HG < 2 else "nq1", "ksvs" if kind == "slc" else "kwvw"]
            return max(job_at[n] for n in need) + 1

        def value_jobs(slot):
            return job_at[{"moba": "mv1", "slc": "ksvs", "win": "vw1"}[slots[slot][0]]] + 1

        block = ctx.enter_context(nc.Block())

        @block.sync
        def _(sp):
            for n in range(NT):
                sp.dma_start(xt[:, n, :], x_v[n]).then_inc(x_in[n], 16)
            for c in (0, 1, 2, 3, 5, 4):
                w = chunk_width[c]
                for half in range(2):
                    sp.dma_start(ring[:, 2 * c + half, 0:4 * w].rearrange("p (k n) -> p k n", k=4),
                                 win_v[:, 4 * half:4 * half + 4, c * CHUNK:c * CHUNK + w])\
                      .then_inc(unit_in[2 * c + half], 16)

            def load_wout(n):
                sp.dma_start(wout[:, 2 * n:2 * n + 2, :], wout_v[:, 2 * n:2 * n + 2, :]).then_inc(wout_in[n], 16)

            def load_unit(e, u):
                if u < UP_UNITS:
                    sp.dma_start(ring[:, u, :], up_v[ds(e, 1), u].rearrange("a p f -> p (a f)"))\
                      .then_inc(unit_in[u], 16)
                else:
                    sp.dma_start(ring[:, u, :].rearrange("p (j d) -> p j d", j=2),
                                 down_v[ds(e, 1), u - UP_UNITS].rearrange("a p j d -> p (a j) d"))\
                      .then_inc(unit_in[u], 16)

            for n in range(1, 4):
                load_wout(n)
            for u in range(UNITS):
                if u == 6:
                    sp.wait_ge(cm1_done, 1)
                    load_wout(0)
                sp.wait_ge(job_done, job_at[last_job_of_chunk[u // 2]] + 1)
                load_unit(0, u)

            def load_expert(i, e):
                for u in range(UP_UNITS):
                    sp.wait_ge(up_used, UP_UNITS * (i - 1) + u + 1)
                    load_unit(e, u)
                for u in range(DOWN_UNITS):
                    sp.wait_ge(down_used, DOWN_UNITS * (i - 1) + u + 1)
                    load_unit(e, UP_UNITS + u)

            with sp.Fori(1, E) as i:
                load_expert(i, i)
            sp.wait_ge(ovi_ready, 1)
            more = sp.value_load(ovi[0:1, 2 * NOV:2 * NOV + 1], min_val=0, max_val=NOV)
            with sp.If(more > 0):
                with sp.Fori(0, more) as o:
                    e = sp.value_load(ovi[0:1, ds(o, 1)], min_val=0, max_val=E - 1)
                    load_expert(o + E, e)
            for n in range(NT):
                sp.wait_ge(fin_ready, n + 1)
                sp.dma_start(out_v[n], xs[:, n, :]).then_inc(out_sent, 16)
            sp.wait_ge(out_sent, 16 * NT)

        @block.gpsimd
        def _(pool):
            chain = [0]

            def link(ins):
                chain[0] += 1
                ins.then_inc(pool_chain, 1)
                pool.wait_ge(pool_chain, chain[0])

            link(pool.memset(ident[:], 0.0))
            pool.affine_select(out=ident[:], in_=ident[:], compare_op=ALU.not_equal, fill=1.0, base=0,
                               pattern=[[-1, P]], channel_multiplier=1).then_inc(ident_ready, 1)
            link(pool.iota(dist, pattern=[[-1, 2 * P]], base=P, channel_multiplier=1,
                           allow_small_or_imprecise_dtypes=True))
            pool.affine_select(out=dist, in_=dist, compare_op=ALU.is_ge, fill=BIG, base=P,
                               pattern=[[-1, 2 * P]], channel_multiplier=1).then_inc(dist_ready, 1)
            pool.wait_ge(dist_ready, 1)
            for h in range(H):
                pool.tensor_scalar(tabs[:, h, :], dist, moba_slope[h], None, ALU.mult).then_inc(tab_ready, 1)
            pool.memset(ones[:], 1.0).then_inc(const_ready, 1)
            pool.memset(upper[:], 1.0).then_inc(const_ready, 1)
            pool.memset(cz, 0.0).then_inc(const_ready, 1)
            pool.memset(hTv[0:HD], 0.0).then_inc(const_ready, 1)
            pool.memset(vc, 0.0).then_inc(const_ready, 1)
            pool.wait_ge(const_ready, 5)
            pool.affine_select(out=upper[:], in_=upper[:], compare_op=ALU.is_gt, fill=0.0, base=0,
                               pattern=[[1, P]], channel_multiplier=-1).then_inc(const_ready, 1)
            link(pool.iota(cdist, pattern=[[P, NT], [-16, 16]], base=-(CMP_L - 1), channel_multiplier=1,
                           allow_small_or_imprecise_dtypes=True))
            link(pool.tensor_scalar(cmask, cdist, 0.0, None, ALU.is_ge))
            link(pool.affine_select(out=cdist, in_=cdist, compare_op=ALU.is_ge, fill=BIG, base=-(CMP_L - 1),
                                    pattern=[[P, NT], [-16, 16]], channel_multiplier=1))
            for h in range(H):
                pool.tensor_scalar(ctab[:, :, h, :], cdist, nsa_slope[h], None, ALU.mult).then_inc(ctab_ready, 1)
            for n, h in enumerate(nsa_order):
                pool.wait_ge(z_done, n + 1)
                pool.tensor_scalar(tabs[:, n, :], dist, nsa_slope[h], None, ALU.mult).then_inc(tab_ready, 1)
            pool.wait_ge(proj_done, NT)
            pool.iota(iota_e, pattern=[[1, E]], base=0, channel_multiplier=0,
                      allow_small_or_imprecise_dtypes=True).then_inc(iotas_ready, 1)
            pool.iota(iota_t, pattern=[[0, 2], [1, TOK]], base=1, channel_multiplier=0,
                      allow_small_or_imprecise_dtypes=True).then_inc(iotas_ready, 1)
            pool.iota(iota_o, pattern=[[1, NOV]], base=0, channel_multiplier=0,
                      allow_small_or_imprecise_dtypes=True).then_inc(iotas_ready, 1)
            pool.iota(more_k, pattern=[[CAP, MORE]], base=CAP, channel_multiplier=0,
                      allow_small_or_imprecise_dtypes=True).then_inc(iotas_ready, 1)
            pool.iota(ecol, pattern=[[0, 1]], base=0, channel_multiplier=1,
                      allow_small_or_imprecise_dtypes=True).then_inc(iotas_ready, 1)
            pool.memset(posp, 0.0).then_inc(iotas_ready, 1)
            pool.memset(Wt, 0.0).then_inc(iotas_ready, 1)
            pool.wait_ge(late_in, 32)
            pool.partition_broadcast(gfin, gfin[0:1, :], P).then_inc(gfin_ready, 1)
            if CAP < 64:
                pool.wait_ge(iotas_ready, 7)
                pool.memset(iota_t[:, CAP:64], -1000.0).then_inc(iotas_ready, 1)
                pool.memset(iota_t[:, 64 + CAP:128], -1000.0).then_inc(iotas_ready, 1)
        IOTAS = 7 if CAP == 64 else 9

        @block.scalar
        def _(act):
            act.dma_start(prm[0:8, :], attn_norm_g.rearrange("o (k p) -> (o k) p", p=P)).then_inc(prm_in, 16)
            act.dma_start(prm[8:16, :], ffn_norm_g.rearrange("o (k p) -> (o k) p", p=P)).then_inc(prm_in, 16)
            act.dma_start(prm[16:32, :], cmp_pe_k.rearrange("o (l t) d -> (o l) (t d)", t=2)).then_inc(prm_in, 16)
            act.dma_start(prm[32:48, :], cmp_pe_v.rearrange("o (l t) d -> (o l) (t d)", t=2)).then_inc(prm_in, 16)
            act.dma_start(w1k, cmp_w1_k.rearrange("o (c p) j -> p (o c) j", p=P)).then_inc(cmpw_in, 16)
            act.dma_start(w1v, cmp_w1_v.rearrange("o (c p) j -> p (o c) j", p=P)).then_inc(cmpw_in, 16)
            act.dma_start(w2k[:], cmp_w2_k[0]).then_inc(cmpw_in, 16)
            act.dma_start(w2v[:], cmp_w2_v[0]).then_inc(cmpw_in, 16)
            act.dma_start(wr[:], w_router.rearrange("o (k p) e -> p (o k) e", p=P)).then_inc(router_in, 16)
            act.dma_start(br[:], b_router[0:1, :].partition_broadcast(P).rearrange("p o e -> p (o e)"))\
               .then_inc(router_in, 16)

            def square(n, j, wait, value):
                act.wait_ge(wait, value)
                act.activation(xs[:, n, :], xt[:, n, :], ACT.Square, accum_out=sq_sum[:, j:j + 1])\
                   .then_inc(squared, 1)

            def sqrt(j):
                act.wait_ge(ms_ready, j + 1)
                act.activation(root[:, j:j + 1], ms[:, j:j + 1], ACT.Sqrt).then_inc(rooted, 1)

            for n in range(NT):
                square(n, n, x_in[n], 16)
                sqrt(n)

            def read_job(name):
                j = job_at[name]
                act.wait_ge(job_done, j + 1)
                b = ps[:, PJ[j % 2], :]
                if name in ("mq0", "mq1", "nq0", "nq1"):
                    dst = (mqT if name[0] == "m" else nqT)[:, 2 * int(name[2]):2 * int(name[2]) + 2, :]
                    act.activation(dst, b.rearrange("p (a q) -> p a q", a=2), ACT.Copy, scale=-HD ** -0.5)\
                       .then_inc(job_read, 1)
                elif name in ("mk0", "mk1"):
                    act.activation(mkT[:, 2 * int(name[2]):2 * int(name[2]) + 2, :],
                                   b.rearrange("p (a q) -> p a q", a=2), ACT.Copy).then_inc(job_read, 1)
                elif name in ("mv0", "mv1"):
                    act.activation(mv[:, int(name[2]), :], b, ACT.Copy).then_inc(job_read, 1)
                elif name == "kcvc":
                    act.wait_ge(r_ready, 4)
                    act.nop().then_inc(job_read, 1)
                elif name == "ksvs":
                    act.activation(ksT, b[:, 0:256], ACT.Copy)
                    act.activation(vs, b[:, 256:512].rearrange("p (t n) -> p t n", t=2), ACT.Copy)\
                       .then_inc(job_read, 1)
                elif name == "kwvw":
                    act.activation(kwT, b[:, 0:256], ACT.Copy)
                    act.activation(vw[:, 0, :], b[:, 256:384], ACT.Copy)
                    act.activation(gtmp[:, 0, :], b[:, 384:408], ACT.Exp, scale=-1.0).then_inc(job_read, 1)
                elif name == "vw1":
                    act.activation(vw[:, 1, :], b[:, 0:128], ACT.Copy)
                    act.activation(gtmp[:, 1, :], b[:, 128:152], ACT.Exp, scale=-1.0).then_inc(job_read, 1)

            for name in pre_jobs:
                read_job(name)
            for s in range(NSLOT + PV_LAG + 1):
                if s >= T_LAG and s - T_LAG < NSLOT:
                    n = s - T_LAG
                    act.wait_ge(pT_done, n + 1)
                    if n >= 2:
                        act.wait_ge(pv_done, n - 1)
                    act.activation(pT[:, n % 2, :], ps[:, TB[n % 2], 0:384], ACT.Copy).then_inc(pT_read, 1)
                if s < NSLOT:
                    act.wait_ge(z_done, s + 1)
                    zb = z[:, s % ZB, :]
                    act.activation(zb[:, 0:128], zb[:, 0:128], ACT.Exp, bias=zmin[:, s % ZB, 0:1], scale=-1.0,
                                   accum_out=zsum[:, s % ZB, 0:1])
                    act.activation(zb[:, 128:384], zb[:, 128:384], ACT.Exp, bias=zmin[:, s % ZB, 1:2], scale=-1.0,
                                   accum_out=zsum[:, s % ZB, 1:2]).then_inc(exp_done, 1)
                if s < len(slot_jobs):
                    read_job(slot_jobs[s])
                if s == CM1_SLOT:
                    act.wait_ge(gelu_t, 1)
                    act.activation(hsq[0:HD, 0:62], ht[0:HD, 0:62], ACT.Exp, scale=-2.0 * 0.7978845608028654)\
                       .then_inc(gelu_exp, 1)
                if s == CM2_SLOT:
                    act.wait_ge(cm2_done, 1)
                    act.activation(kcT[:, 0:NC], ps[:, PJ[1], 0:NC], ACT.Copy)
                    act.wait_ge(const_ready, 6)
                    for a in range(HG):
                        k = slice(32 * a, 32 * a + 32)
                        t = act.activation(vc[k, :, a * HD:(a + 1) * HD],
                                           ps[k, PJ[1], 64:192].rearrange("p (g d) -> p g d", g=2), ACT.Copy)
                    t.then_inc(cm2_read, 1)
                if s == CS_SLOT:
                    act.wait_ge(cz_ready, 1)
                    act.activation(cz[:, :, :, 0:NC], cz[:, :, :, 0:NC], ACT.Exp, scale=-1.0).then_inc(cexp_done, 1)
                if s == CT_SLOT:
                    act.wait_ge(cpT_done, 1)
                    act.activation(pcT, ps[:, PJ[1], :].rearrange("p (a q) -> p a q", a=4), ACT.Copy)\
                       .then_inc(cpT_read, 1)

            for b in range(4):
                act.wait_ge(xT_ps, 4 + b + 1)
                n, half = b // 2, b % 2
                act.activation(xT[:, 4 * half:4 * half + 4, n * P:(n + 1) * P],
                               ps[:, PJ[b % 2], :].rearrange("p (k q) -> p k q", k=4), ACT.Copy).then_inc(xT_ready, 1)

            for n in range(NT):
                square(n, 2 + n, x2_ready, n + 1)
                sqrt(2 + n)
            act.dma_start(bd[0:E, :], b_down[0]).then_inc(late_in, 16)
            act.dma_start(gfin[0:1, :], final_norm_g.rearrange("(o d) -> o d", o=1)).then_inc(late_in, 16)
            act.dma_start(brow[0:1, :], bup_v[0:1, :]).then_inc(brow_in, 16)
            act.wait_ge(td_ready, 1)
            act.activation(texp, tdiff, ACT.Exp).then_inc(te_ready, 1)

            def read_xg(b):
                act.wait_ge(xg_done, b + 1)
                act.activation(xg, ps[:, XG, :], ACT.Copy).then_inc(xg_read, 1)

            def sigmoid(b):
                act.wait_ge(swi, b * 3 + 1)
                act.activation(t2, t1, ACT.Sigmoid, scale=1.702).then_inc(sig_done, 1)

            def read_rest(b, prev):
                act.wait_ge(cT_done, b + 1)
                if prev:
                    act.wait_ge(comb_done, b)
                act.activation(cT, ps[:, XG, 0:256].rearrange("p (n q) -> p n q", n=2), ACT.Copy).then_inc(cT_read, 1)
                act.wait_ge(aT_done, b + 1)
                act.activation(aT[:, 0:2, :], UP[:, 0, 0:256].rearrange("p (a q) -> p a q", a=2), ACT.Copy)\
                   .then_inc(aT_read, 1)
                act.wait_ge(down_used, b * DOWN_UNITS + DOWN_UNITS)
                act.activation(yv, ps[:, XG, :], ACT.Copy).then_inc(y_read, 1)

            def load_brow(b, e):
                act.wait_ge(bias_used, b)
                act.dma_start(brow[0:1, :], bup_v[ds(e, 1), :]).then_inc(brow_in, 16)

            read_xg(0)
            load_brow(1, 1)
            act.wait_ge(wT_done, 1)
            act.activation(WT[0:E, :], ps[0:E, OUT[0][1], 128:384], ACT.Copy).then_inc(wT_read, 1)
            sigmoid(0)
            read_xg(1)
            read_rest(0, False)
            with act.Fori(1, E - 1) as i:
                load_brow(i + 1, i + 1)
                sigmoid(i)
                read_xg(i + 1)
                read_rest(i, True)
            sigmoid(E - 1)
            read_rest(E - 1, True)
            act.wait_ge(ovi_ready, 1)
            more = act.value_load(ovi[0:1, 2 * NOV:2 * NOV + 1], min_val=0, max_val=NOV)
            with act.If(more > 0):
                with act.Fori(0, more) as o:
                    e = act.value_load(ovi[0:1, ds(o, 1)], min_val=0, max_val=E - 1)
                    load_brow(o + E, e)
                    read_xg(o + E)
                    sigmoid(o + E)
                    read_rest(o + E, True)

            for n in range(NT):
                square(n, 4 + n, x2_ready, NT + n + 1)
                sqrt(4 + n)

        @block.tensor
        def _(pe):
            pe.wait_ge(ident_ready, 1)
            pe.wait_ge(prm_in, 64)
            pe.transpose(ps[:, PJ[0], 0:48], prm[:, :], ident[0:48, 0:48]).then_inc(prmT_ps, 1)

            def transposes(n, k0, bank):
                for k in range(4):
                    t = pe.transpose(ps[:, bank, k * P:(k + 1) * P], xs[:, n, (k0 + k) * P:(k0 + k + 1) * P],
                                     ident[:, :])
                t.then_inc(xT_ps, 1)

            for n in range(NT):
                pe.wait_ge(xs_ready, n + 1)
                for half in range(2):
                    b = 2 * n + half
                    if b == 0:
                        pe.wait_ge(prmT_ready, 1)
                    if b >= 2:
                        pe.wait_ge(xT_ready, b - 1)
                    transposes(n, 4 * half, PJ[half])
            pe.wait_ge(xT_ready, 4)

            def across(dst, c, lhs):
                for k in range(KD):
                    pe.wait_ge(unit_in[2 * c + k // 4], 16)
                    t = pe.matmul(dst, lhs(win_unit(c, k)), xT[:, k, :], start=(k == 0), stop=(k == KD - 1))
                return t

            def along(dst, c, n, lo, hi):
                for k in range(KD):
                    pe.wait_ge(unit_in[2 * c + k // 4], 16)
                    t = pe.matmul(dst, xT[:, k, n * P:(n + 1) * P], win_unit(c, k)[:, lo:hi],
                                  start=(k == 0), stop=(k == KD - 1))
                return t

            def job(name):
                j = job_at[name]
                if j >= 2:
                    pe.wait_ge(job_read, j - 1)
                b = ps[:, PJ[j % 2], :]
                if name[:2] in ("mq", "mk"):
                    for a in range(2):
                        o = (2 * int(name[2]) + a) * P
                        t = across(b[:, a * S:(a + 1) * S], 0 if name[1] == "q" else 1, lambda w: w[:, o:o + P])
                elif name[:2] == "mv":
                    t = along(b, 2, int(name[2]), 0, 512)
                elif name[:2] == "nq":
                    for a in range(2):
                        o = (2 * int(name[2]) + a) * HD
                        for k in range(KD):
                            pe.wait_ge(unit_in[6 + k // 4], 16)
                            for g in range(G):
                                t = pe.matmul(b[g * HD:(g + 1) * HD, a * S:(a + 1) * S],
                                              win_unit(3, k)[:, g * S + o:g * S + o + HD], xT[:, k, :],
                                              start=(k == 0), stop=(k == KD - 1), skip_group_check=True)
                elif name == "kcvc":
                    for a in range(2):
                        t = across(b[:, a * S:(a + 1) * S], 4, lambda w: w[:, a * P:(a + 1) * P])
                elif name == "ksvs":
                    across(b[:, 0:S], 4, lambda w: w[:, 2 * P:3 * P])
                    for n in range(NT):
                        t = along(b[:, S + n * P:S + (n + 1) * P], 4, n, 3 * P, 4 * P)
                elif name == "kwvw":
                    across(b[:, 0:S], 5, lambda w: w[:, 0:P])
                    t = along(b[:, S:S + 152], 5, 0, P, 280)
                elif name == "vw1":
                    t = along(b[:, 0:152], 5, 1, P, 280)
                t.then_inc(job_done, 1)

            def scores(s):
                qT, kT, _, _ = head_of(s)
                pe.wait_ge(job_read, score_jobs(s))
                if s >= 2:
                    pe.wait_ge(z_done, s - 1)
                b = ps[:, SB[s % 2], :]
                pe.matmul(b[:, 0:P], qT[:, 0:P], kT[:, 0:P], start=True, stop=True)
                pe.matmul(b[:, P:P + S], qT[:, P:S], kT, start=True, stop=True).then_inc(s_done, 1)

            def turn(s):
                pe.wait_ge(p_scaled, s + 1)
                if s >= 2:
                    pe.wait_ge(pT_read, s - 1)
                for k in range(3):
                    t = pe.transpose(ps[:, TB[s % 2], k * P:(k + 1) * P], z[:, s % ZB, (0, P, 2 * P)[k]:][:, 0:P],
                                     ident[:, :])
                t.then_inc(pT_done, 1)

            def values(s):
                _, _, v, o = head_of(s)
                pe.wait_ge(job_read, value_jobs(s))
                pe.wait_ge(pT_read, s + 1)
                if s == H:
                    pe.wait_ge(o_read, 1)
                first = s in (0, H)
                p = pT[:, s % 2, :]
                pe.matmul(ps[:, OB[0], o:o + HD], p[:, 0:P], v(0), start=first, stop=True, skip_group_check=True)
                pe.matmul(ps[:, OB[1], o:o + HD], p[:, P:2 * P], v(0), start=first, stop=False,
                          skip_group_check=True)
                pe.matmul(ps[:, OB[1], o:o + HD], p[:, 2 * P:3 * P], v(1), start=False, stop=True,
                          skip_group_check=True).then_inc(pv_done, 1)

            for name in pre_jobs:
                job(name)
            for s in range(NSLOT + PV_LAG + 1):
                if s < NSLOT:
                    scores(s)
                if s >= T_LAG and s - T_LAG < NSLOT:
                    turn(s - T_LAG)
                if s >= PV_LAG and s - PV_LAG < NSLOT:
                    values(s - PV_LAG)
                if s < len(slot_jobs):
                    job(slot_jobs[s])
                if s == CM1_SLOT:
                    pe.wait_ge(job_read, len(jobs))
                    pe.wait_ge(cmpw_in, 64)
                    pe.wait_ge(r_ready, 4)
                    for i, w in enumerate((w1k, w1v)):
                        for c in range(LP):
                            t = pe.matmul(ps[0:HD, PJ[0], 32 * i:32 * i + 30], w[:, c, :],
                                          R[i][:, :, c, :], start=(c == 0), stop=(c == LP - 1))
                    t.then_inc(cm1_done, 1)
                if s == CM2_SLOT:
                    pe.wait_ge(gelu_done, 2)
                    for g in range(G):
                        pe.matmul(ps[g * HD:(g + 1) * HD, PJ[1], 0:NC], w2k[:], hTk[0:HD, g * NC:(g + 1) * NC],
                                  start=True, stop=True)
                    for g in range(G):
                        t = pe.matmul(ps[:, PJ[1], 64 + g * HD:64 + (g + 1) * HD],
                                      hTv[0:HD, g].rearrange("p a n -> p (a n)"), w2v[:], start=True, stop=True)
                    t.then_inc(cm2_done, 1)
                if s == CS_SLOT:
                    pe.wait_ge(cm2_read, 1)
                    for n in range(NT):
                        for h in range(H):
                            b = (h // HG) * HD
                            o = (n * HG + h % HG) * 32
                            t = pe.matmul(ps[:, PJ[h // HG], o:o + NC], nqT[b:b + HD, h % HG, n * P:(n + 1) * P],
                                          kcT[b:b + HD, 0:NC], start=True, stop=True)
                    t.then_inc(cs_done, 1)
                if s == CT_SLOT:
                    pe.wait_ge(cp_ready, 1)
                    for a in range(4):
                        t = pe.transpose(ps[:, PJ[1], a * P:(a + 1) * P],
                                         cz[:, a // 2, 4 * (a % 2):4 * (a % 2) + 4, :].rearrange("p h c -> p (h c)"),
                                         ident[:, :])
                    t.then_inc(cpT_done, 1)
            pe.wait_ge(cpT_read, 1)
            for n in range(NT):
                for g in range(G):
                    t = pe.matmul(ps[:, OB[n], g * 256:(g + 1) * 256], pcT[:, 2 * n + g, :], vc[:, g, :],
                                  start=False, stop=True, skip_group_check=True)
            t.then_inc(pv_done, 1)

            for b in range(4):
                n, half = b // 2, b % 2
                pe.wait_ge(o_read, 1 if half == 0 else 2)
                if b >= 2:
                    pe.wait_ge(xT_ready, 4 + b - 1)
                transposes(n, 4 * half, PJ[half])
            for n in range(NT):
                pe.wait_ge(xT_ready, 4 + 2 * n + 2)
                for half in range(2):
                    for k in range(KD):
                        pe.wait_ge(wout_in[k // 2], 16)
                        t = pe.matmul(ps[:, 2 + 2 * n + half, :], xT[:, k, n * P:(n + 1) * P],
                                      wout[:, k, half * 512:(half + 1) * 512], start=(k == 0), stop=(k == KD - 1))
                t.then_inc(proj_done, 1)

            for b in range(4):
                n, half = b // 2, b % 2
                pe.wait_ge(xs_ready, NT + n + 1)
                if b >= 2:
                    pe.wait_ge(xT_ready, 8 + b - 1)
                transposes(n, 4 * half, PJ[half])
            pe.wait_ge(router_in, 32)
            for n in range(NT):
                pe.wait_ge(xT_ready, 8 + 2 * n + 2)
                for k in range(KD):
                    t = pe.matmul(ps[:, OUT[1][0], n * E:(n + 1) * E], xT[:, k, n * P:(n + 1) * P], wr[:, k, :],
                                  start=(k == 0), stop=(k == KD - 1))
            t.then_inc(logits_done, 1)
            pe.wait_ge(m_ready, 1)
            pe.wait_ge(const_ready, 6)
            b = ps[:, OUT[1][1], :]
            pe.matmul(b[:, 0:E], upper[:], M[:, 0, :], start=True, stop=True)
            pe.matmul(b[:, E:2 * E], ones[:], M[:, 0, :], start=True, stop=False)
            pe.matmul(b[:, E:2 * E], upper[:], M[:, 1, :], start=False, stop=True)
            for n in range(NT):
                t = pe.matmul(b[0:E, 64:65], M[:, n, :], ones[:, 0:1], start=(n == 0), stop=(n == 1))
            t.then_inc(pos_done, 1)

            def gather(b, first=False):
                pe.wait_ge(pm_ready, b + 1)
                if not first:
                    pe.wait_ge(y_read, b - 1)
                for n in range(NT):
                    for h in range(2):
                        t = pe.matmul(ps[h * 64:(h + 1) * 64, XG, :], pm[:, n, :], xs[:, n, h * 512:(h + 1) * 512],
                                      start=(n == 0), stop=(n == 1), skip_group_check=True)
                t.then_inc(xg_done, 1)

            def gather_turn(b):
                pe.wait_ge(xg_read, b + 1)
                for j in range(4):
                    t = pe.transpose(ps[:, XTB, j * P:(j + 1) * P], xg[:, j * P:(j + 1) * P], ident[:, :])
                t.then_inc(xgT_done, 1)

            def up(b, prev):
                pe.wait_ge(xgT_read, b + 1)
                pe.wait_ge(brow_in, b * 16 + 16)
                if prev:
                    pe.wait_ge(aT_read, b * 2)
                for c in range(4):
                    t = pe.matmul(UP[(c % 2) * 64:(c % 2) * 64 + 64, c // 2, :], ones[0:1, 0:64],
                                  brow[0:1, c * 512:(c + 1) * 512], start=True, stop=False, skip_group_check=True)
                t.then_inc(bias_used, 1)
                for k in range(KD):
                    pe.wait_ge(unit_in[k], b * 16 + 32)
                    for c in range(4):
                        t = pe.matmul(UP[(c % 2) * 64:(c % 2) * 64 + 64, c // 2, :], xgT[:, k, :],
                                      ring[:, k, c * 512:(c + 1) * 512], start=False, stop=(k == KD - 1),
                                      skip_group_check=True)
                    t.then_inc(up_used, 1)

            def combine_turn(b, ahead):
                pe.wait_ge(pw_ready, b + 1)
                pe.wait_ge(xg_read, b + 1 + ahead)
                for n in range(NT):
                    t = pe.transpose(ps[:, XG, n * P:(n + 1) * P], pw[:, n, :], ident[:, :])
                t.then_inc(cT_done, 1)

            def act_turn(b):
                pe.wait_ge(a_ready, b + 1)
                for j in range(4):
                    t = pe.transpose(UP[:, j // 2, (j % 2) * P:(j % 2 + 1) * P], av[:, j // 2, (j % 2) * P:(j % 2 + 1) * P],
                                     ident[:, :])
                t.then_inc(aT_done, 1)

            def down(b):
                pe.wait_ge(aT_read, b * 2 + 2)
                pe.wait_ge(cT_read, b + 1)
                for u in range(DOWN_UNITS):
                    pe.wait_ge(unit_in[UP_UNITS + u], b * 16 + 32)
                    for j in range(2):
                        for h in range(2):
                            t = pe.matmul(ps[h * 64:(h + 1) * 64, XG, :],
                                          aT[:, 2 * (u // 2) + j, (u % 2) * 64:(u % 2) * 64 + 64],
                                          ring[:, UP_UNITS + u, j * D + h * 512:j * D + (h + 1) * 512],
                                          start=(u == 0 and j == 0), stop=(u == DOWN_UNITS - 1 and j == 1),
                                          skip_group_check=True)
                    t.then_inc(down_used, 1)

            def combine(b):
                pe.wait_ge(y_read, b + 1)
                for n in range(NT):
                    for h in range(2):
                        t = pe.matmul(ps[:, OUT[n][h], :], cT[h * 64:(h + 1) * 64, n, :], yv[h * 64:(h + 1) * 64, :],
                                      start=False, stop=True, skip_group_check=True)
                t.then_inc(comb_done, 1)

            gather(0, first=True)
            gather_turn(0)
            pe.wait_ge(w_ready, 1)
            for n in range(NT):
                t = pe.transpose(ps[0:E, OUT[0][1], P + n * P:P + (n + 1) * P], Wt[:, n, 0:E], ident[:, :])
            t.then_inc(wT_done, 1)
            pe.wait_ge(nflag_ready, 1)
            pe.matmul(ps[0:E, OUT[0][0], 0:1], upper[0:E, 0:E], nflag[0:E], start=True, stop=True)\
              .then_inc(rank_done, 1)
            pe.wait_ge(rsel_ready, 3)
            b = ps[:, OUT[0][0], :]
            pe.matmul(b[:, 64:64 + NOV], ones[0:E, :], Re[0:E, :], start=True, stop=True)
            pe.matmul(b[:, 64 + NOV:64 + 2 * NOV], ones[0:E, :], Rb[0:E, :], start=True, stop=True)
            pe.matmul(b[:, 64 + 2 * NOV:65 + 2 * NOV], ones[0:E, :], nflag[0:E], start=True, stop=True)\
              .then_inc(ovt_done, 1)

            up(0, False)
            gather(1, first=True)
            pe.wait_ge(wT_read, 1)
            pe.wait_ge(ovi_ready, 1)
            pe.wait_ge(late_in, 32)
            for n in range(NT):
                for h in range(2):
                    pe.matmul(ps[:, OUT[n][h], :], WT[0:E, n * P:(n + 1) * P], bd[0:E, h * 512:(h + 1) * 512],
                              start=True, stop=False, skip_group_check=True)
            combine_turn(0, 1)
            gather_turn(1)
            act_turn(0)
            down(0)
            with pe.Fori(1, E - 1) as i:
                up(i, True)
                gather(i + 1)
                combine(i - 1)
                combine_turn(i, 1)
                gather_turn(i + 1)
                act_turn(i)
                down(i)
            up(E - 1, True)
            combine(E - 2)
            combine_turn(E - 1, 0)
            act_turn(E - 1)
            down(E - 1)
            combine(E - 1)
            more = pe.value_load(ovi[0:1, 2 * NOV:2 * NOV + 1], min_val=0, max_val=NOV)
            with pe.If(more > 0):
                with pe.Fori(0, more) as o:
                    gather(o + E)
                    gather_turn(o + E)
                    up(o + E, True)
                    combine_turn(o + E, 0)
                    act_turn(o + E)
                    down(o + E)
                    combine(o + E)

        @block.vector
        def _(dve):
            chain = [0]

            def link(ins):
                chain[0] += 1
                ins.then_inc(dve_chain, 1)
                dve.wait_ge(dve_chain, chain[0])

            def norm(n, j, ready=None):
                dve.wait_ge(squared, j + 1)
                dve.tensor_scalar(ms[:, j:j + 1], sq_sum[:, j:j + 1], 1.0 / D, EPS, ALU.mult, ALU.add)\
                   .then_inc(ms_ready, 1)
                dve.wait_ge(rooted, j + 1)
                link(dve.reciprocal(rstd[:, j:j + 1], root[:, j:j + 1]))
                if j < 4:
                    dve.tensor_scalar(xs[:, n, :], xt[:, n, :], rstd[:, j:j + 1], None, ALU.mult)\
                       .then_inc(xs_ready, 1)

            def read_xT(b, base, gain):
                n, half = b // 2, b % 2
                dve.wait_ge(xT_ps, base + b + 1)
                dve.tensor_tensor(xT[:, 4 * half:4 * half + 4, n * P:(n + 1) * P],
                                  ps[:, PJ[half], :].rearrange("p (k q) -> p k q", k=4),
                                  gain[:, 4 * half:4 * half + 4].unsqueeze(2).broadcast_to([P, 4, P]),
                                  ALU.mult).then_inc(xT_ready, 1)

            dve.wait_ge(prmT_ps, 1)
            dve.tensor_copy(prmT[:, :], ps[:, PJ[0], 0:48]).then_inc(prmT_ready, 1)
            dve.wait_ge(prmT_ready, 1)
            for n in range(NT):
                norm(n, n)
                read_xT(2 * n, 0, gaT)
                read_xT(2 * n + 1, 0, gaT)

            def scale_p(s):
                kind, h = slots[s]
                dve.wait_ge(exp_done, s + 1)
                q = s % ZB
                link(dve.tensor_scalar(zrec[:, q, :], zsum[:, q, :], 1e-30, None, ALU.max))
                link(dve.reciprocal(zrec[:, q, :], zrec[:, q, :]))
                for n, (a, b) in enumerate(((0, 128), (128, 384))):
                    gate = {"moba": None, "slc": 1, "win": 2}[kind]
                    zb = z[:, q, a:b]
                    if gate is None:
                        t = dve.tensor_scalar(zb, zb, zrec[:, q, n:n + 1], None, ALU.mult)
                    else:
                        c = 3 * h + gate
                        t = dve.tensor_scalar(zb, zb, zrec[:, q, n:n + 1], gates[:, n, c:c + 1], ALU.mult, ALU.mult)
                t.then_inc(p_scaled, 1)

            for s in range(NSLOT + PV_LAG + 1):
                if s < NSLOT:
                    q = s % ZB
                    dve.wait_ge(s_done, s + 1)
                    dve.wait_ge(tab_ready, s % H + 1 + (H if s >= H else 0))
                    if s >= ZB:
                        dve.wait_ge(pT_done, s - ZB + 1)
                    b = ps[:, SB[s % 2], :]
                    dve.tensor_tensor_reduce(z[:, q, 0:P], b[:, 0:P], tabs[:, s % H, P:2 * P], 1.0, 3e38,
                                             ALU.add, ALU.min, zmin[:, q, 0:1])
                    dve.tensor_tensor_reduce(z[:, q, P:3 * P], b[:, P:3 * P], tabs[:, s % H, :], 1.0, 3e38,
                                             ALU.add, ALU.min, zmin[:, q, 1:2]).then_inc(z_done, 1)
                if 1 <= s and s - 1 < NSLOT:
                    scale_p(s - 1)
                if s < len(slot_jobs) and slot_jobs[s] == "kcvc":
                    j = job_at["kcvc"]
                    dve.wait_ge(job_done, j + 1)
                    for i in range(2):
                        for lp in range(2):
                            for g in range(G):
                                src = ps[g * HD:(g + 1) * HD, PJ[j % 2], i * S:(i + 1) * S]
                                v = cmp_tokens(src, lp)
                                t = dve.tensor_tensor(
                                    R[i][lp * HD:(lp + 1) * HD, g, :, :], v,
                                    peT[i][lp * HD:(lp + 1) * HD, :].unsqueeze(2).broadcast_to([HD, LP, NC]),
                                    ALU.add)
                            t.then_inc(r_ready, 1)
                if s == H - 1:
                    dve.wait_ge(job_read, job_at["vw1"] + 1)
                    link(dve.tensor_scalar(gtmp, gtmp, 1.0, None, ALU.add))
                    link(dve.reciprocal(gates, gtmp))
                if s == CM1_SLOT:
                    dve.wait_ge(cm1_done, 1)
                    k = slice(0, HD)
                    link(dve.memset(hx[k, 0:62], 0.0))
                    dve.tensor_copy(hx[k, 0:30], ps[k, PJ[0], 0:30])
                    link(dve.tensor_copy(hx[k, 32:62], ps[k, PJ[0], 32:62]))
                    link(dve.tensor_tensor(hsq[k, 0:62], hx[k, 0:62], hx[k, 0:62], ALU.mult))
                    link(dve.tensor_scalar(hsq[k, 0:62], hsq[k, 0:62], 0.044715, 1.0, ALU.mult, ALU.add))
                    dve.tensor_tensor(ht[k, 0:62], hsq[k, 0:62], hx[k, 0:62], ALU.mult).then_inc(gelu_t, 1)
                if s == CM1_SLOT + 1:
                    dve.wait_ge(gelu_exp, 1)
                    k = slice(0, HD)
                    link(dve.tensor_scalar(hsq[k, 0:62], hsq[k, 0:62], 1.0, None, ALU.add))
                    link(dve.reciprocal(hsq[k, 0:62], hsq[k, 0:62]))
                    dve.tensor_tensor(hTk[k, 0:30], hsq[k, 0:30], hx[k, 0:30], ALU.mult).then_inc(gelu_done, 1)
                    dve.wait_ge(const_ready, 6)
                    for g in range(G):
                        o = 32 + NC * g
                        t = dve.tensor_tensor(hTv[k, g, :, 0:NC],
                                              hsq[k, o:o + NC].unsqueeze(1).broadcast_to([HD, 4, NC]),
                                              hx[k, o:o + NC].unsqueeze(1).broadcast_to([HD, 4, NC]), ALU.mult)
                    t.then_inc(gelu_done, 1)
                if s == CS_SLOT:
                    dve.wait_ge(cs_done, 1)
                    dve.wait_ge(ctab_ready, H)
                    cv = cz[:, :, :, 0:NC]
                    for g in range(G):
                        hs = slice(HG * g, HG * g + HG)
                        t = dve.tensor_tensor(cz[:, :, hs, 0:NC],
                                              ps[:, PJ[g], 0:256].rearrange("p (n h c) -> p n h c", n=2, h=HG)[:, :, :, 0:NC],
                                              ctab[:, :, hs, 0:NC], ALU.add)
                    link(t)
                    link(dve.tensor_reduce(cmin, cv, AX.X, ALU.min))
                    dve.tensor_tensor(cv, cv, cmin.unsqueeze(3).broadcast_to([P, 2, H, NC]), ALU.subtract)\
                       .then_inc(cz_ready, 1)
                if s == CS_SLOT + 1:
                    dve.wait_ge(cexp_done, 1)
                    cv = cz[:, :, :, 0:NC]
                    link(dve.tensor_tensor(cv, cv, cmask[:, :, 0:NC].unsqueeze(2).broadcast_to([P, 2, H, NC]),
                                           ALU.mult))
                    link(dve.tensor_reduce(csum, cv, AX.X, ALU.add))
                    link(dve.tensor_scalar(csum, csum, 1e-30, None, ALU.max))
                    link(dve.reciprocal(crec, csum))
                    link(dve.tensor_tensor(crec, crec, gates.rearrange("p n (h b) -> p n h b", b=3)[:, :, :, 0],
                                           ALU.mult))
                    dve.tensor_tensor(cv, cv, crec.unsqueeze(3).broadcast_to([P, 2, H, NC]), ALU.mult)\
                       .then_inc(cp_ready, 1)
                if s == H - 1 + PV_LAG:
                    dve.wait_ge(pv_done, H)
                    dve.tensor_copy(xs[:, :, 0:512], ps[:, OB[0]:OB[1] + 1, :]).then_inc(o_read, 1)
            dve.wait_ge(pv_done, NSLOT + 1)
            dve.tensor_copy(xs[:, :, 512:1024], ps[:, OB[0]:OB[1] + 1, :]).then_inc(o_read, 1)

            for n in range(NT):
                dve.wait_ge(proj_done, n + 1)
                dve.tensor_tensor(xt[:, n, :].rearrange("p (h q) -> p h q", h=2), ps[:, 2 + 2 * n:4 + 2 * n, :],
                                  xt[:, n, :].rearrange("p (h q) -> p h q", h=2), ALU.add).then_inc(x2_ready, 1)
                norm(n, 2 + n)
            for b in range(4):
                read_xT(b, 8, gfT)

            dve.wait_ge(logits_done, 1)
            dve.wait_ge(router_in, 32)
            dve.wait_ge(iotas_ready, IOTAS)
            link(dve.tensor_tensor(lg, ps[:, OUT[1][0], 0:2 * E].rearrange("p (n e) -> p n e", n=2),
                                   br[:, :].unsqueeze(1).broadcast_to([P, 2, E]), ALU.add))
            dve.max(top[:, 0, :], lg[:, 0, :])
            link(dve.max(top[:, 1, :], lg[:, 1, :]))
            dve.max_index(topi[:, 0, :], top[:, 0, :], lg[:, 0, :])
            link(dve.max_index(topi[:, 1, :], top[:, 1, :], lg[:, 1, :]))
            link(dve.tensor_copy(topf, topi[:, :, 0:TOPK]))
            hot_v = hot.rearrange("p n k e -> p (n k) e")
            link(dve.tensor_tensor(hot_v, iota_e.unsqueeze(1).broadcast_to([P, 2 * TOPK, E]),
                                   topf.rearrange("p n k -> p (n k)").unsqueeze(2).broadcast_to([P, 2 * TOPK, E]),
                                   ALU.is_equal))
            dve.tensor_reduce(M, hot.rearrange("p n k e -> p n e k"), AX.X, ALU.add).then_inc(m_ready, 1)
            dve.tensor_tensor(tdiff, top[:, :, 0:TOPK], top[:, :, 0:1].broadcast_to([P, 2, TOPK]), ALU.subtract)\
               .then_inc(td_ready, 1)
            dve.wait_ge(m_ready, 1)
            dve.wait_ge(pos_done, 1)
            b = ps[:, OUT[1][1], :]
            link(dve.scalar_tensor_tensor(out=posp[:, :, 0:E], in0=b[:, 0:2 * E].rearrange("p (n e) -> p n e", n=2),
                                          scalar=1.0, in1=M, op0=ALU.add, op1=ALU.mult))

            def pick(b, e, base=None, first=False):
                if not first:
                    dve.wait_ge(pw_ready, b)
                if base is None:
                    dve.tensor_scalar(pcol, posp[:, :, ds(e, 1)].rearrange("p n o -> p (n o)"), 0.0, None,
                                      ALU.subtract).then_inc(pcol_ready, 1)
                else:
                    dve.tensor_scalar(pcol, posp[:, :, ds(e, 1)].rearrange("p n o -> p (n o)"), base, None,
                                      ALU.subtract).then_inc(pcol_ready, 1)
                dve.wait_ge(pcol_ready, b + 1)
                for n in range(NT):
                    t = dve.tensor_scalar(pm[:, n, :], iota_t[:, 0:64], pcol[:, n:n + 1], None, ALU.is_equal)
                t.then_inc(pm_ready, 1)

            def weigh(b, e):
                for n in range(NT):
                    t = dve.tensor_scalar(pw[:, n, :], iota_t, pcol[:, n:n + 1],
                                          Wt[:, n, ds(e, 1)], ALU.is_equal, ALU.mult)
                t.then_inc(pw_ready, 1)

            def read_xgT(b):
                dve.wait_ge(xgT_done, b + 1)
                dve.tensor_tensor(xgT.rearrange("p (h j) t -> p j h t", h=2),
                                  ps[:, XTB, :].rearrange("p (j h t) -> p j h t", j=4, h=2),
                                  gfT.rearrange("p (h j) -> p j h", h=2).unsqueeze(3).broadcast_to([P, 4, 2, 64]),
                                  ALU.mult).then_inc(xgT_read, 1)

            def swiglu(b, between=None):
                dve.wait_ge(up_used, b * UP_UNITS + UP_UNITS)
                dve.tensor_scalar(t1, UP[:, :, 0:512:2], 7.0, None, ALU.min).then_inc(swi, 1)
                dve.tensor_scalar(t3, UP[:, :, 1:512:2], 7.0, -1000.0, ALU.min, ALU.max).then_inc(swi, 1)
                dve.wait_ge(swi, b * 3 + 2)
                dve.scalar_tensor_tensor(out=t3, in0=t3, scalar=1.0, in1=t1, op0=ALU.add, op1=ALU.mult)\
                   .then_inc(swi, 1)
                dve.wait_ge(swi, b * 3 + 3)
                dve.wait_ge(sig_done, b + 1)
                dve.tensor_tensor(av, t3, t2, ALU.mult).then_inc(a_ready, 1)

            def read_aT(b):
                dve.wait_ge(aT_done, b + 1)
                dve.tensor_copy(aT[:, 2:4, :], UP[:, 1, 0:256].rearrange("p (a q) -> p a q", a=2))\
                   .then_inc(aT_read, 1)

            pick(0, 0, first=True)
            read_xgT(0)
            dve.wait_ge(te_ready, 1)
            link(dve.tensor_reduce(tsum, texp, AX.X, ALU.add))
            link(dve.reciprocal(trec, tsum))
            link(dve.tensor_tensor(tw, texp, trec.unsqueeze(2).broadcast_to([P, 2, TOPK]), ALU.mult))
            link(dve.tensor_tensor(hotw.rearrange("p n k e -> p (n k) e"), hot_v,
                                   tw.rearrange("p n k -> p (n k)").unsqueeze(2).broadcast_to([P, 2 * TOPK, E]),
                                   ALU.mult))
            dve.tensor_reduce(Wt[:, :, 0:E], hotw.rearrange("p n k e -> p n e k"), AX.X, ALU.add)\
               .then_inc(w_ready, 1)
            link(dve.tensor_copy(cnt[0:E], b[0:E, 64:65]))
            link(dve.tensor_tensor(flag[0:E], cnt[0:E].broadcast_to([E, MORE]), more_k[0:E], ALU.is_gt))
            dve.tensor_reduce(nflag[0:E], flag[0:E], AX.X, ALU.add).then_inc(nflag_ready, 1)
            dve.wait_ge(rank_done, 1)
            link(dve.tensor_copy(cnt[0:E], ps[0:E, OUT[0][0], 0:1]))
            link(dve.tensor_scalar(rank[0:E], more_k[0:E], 1.0 / CAP, -1.0, ALU.mult, ALU.add))
            link(dve.tensor_scalar(rank[0:E], rank[0:E], cnt[0:E], None, ALU.add))
            link(dve.tensor_tensor(Rsel[0:E], iota_o[0:E].unsqueeze(1).broadcast_to([E, MORE, NOV]),
                                   rank[0:E].unsqueeze(2).broadcast_to([E, MORE, NOV]), ALU.is_equal))
            link(dve.tensor_tensor(Rsel[0:E], Rsel[0:E], flag[0:E].unsqueeze(2).broadcast_to([E, MORE, NOV]),
                                   ALU.mult))
            link(dve.tensor_reduce(Rk[0:E], Rsel[0:E].rearrange("p k i -> p i k"), AX.X, ALU.add))
            dve.tensor_scalar(Re[0:E], Rk[0:E], ecol[0:E], None, ALU.mult).then_inc(rsel_ready, 1)
            link(dve.tensor_tensor(Rsel[0:E], Rsel[0:E], more_k[0:E].unsqueeze(2).broadcast_to([E, MORE, NOV]),
                                   ALU.mult))
            dve.tensor_reduce(Rb[0:E], Rsel[0:E].rearrange("p k i -> p i k"), AX.X, ALU.add)\
               .then_inc(rsel_ready, 2)
            dve.wait_ge(ovt_done, 1)
            link(dve.tensor_copy(ovt, ps[:, OUT[0][0], 64:65 + 2 * NOV]))
            dve.tensor_copy(ovi, ovt).then_inc(ovi_ready, 1)

            dve.wait_ge(w_ready, 1)
            weigh(0, 0)
            dve.wait_ge(xg_done, 1)
            pick(1, 1)
            swiglu(0)
            read_xgT(1)
            read_aT(0)
            with dve.Fori(1, E - 1) as i:
                dve.wait_ge(cT_done, i)
                weigh(i, i)
                dve.wait_ge(xg_done, i + 1)
                pick(i + 1, i + 1)
                swiglu(i)
                read_xgT(i + 1)
                read_aT(i)
            dve.wait_ge(cT_done, E - 1)
            weigh(E - 1, E - 1)
            swiglu(E - 1)
            read_aT(E - 1)
            more = dve.value_load(ovi[0:1, 2 * NOV:2 * NOV + 1], min_val=0, max_val=NOV)
            with dve.If(more > 0):
                with dve.Fori(0, more) as o:
                    e = dve.value_load(ovi[0:1, ds(o, 1)], min_val=0, max_val=E - 1)
                    dve.wait_ge(xg_done, o + E)
                    dve.wait_ge(cT_done, o + E)
                    pick(o + E, e, ovt[:, ds(o + NOV, 1)])
                    weigh(o + E, e)
                    read_xgT(o + E)
                    swiglu(o + E)
                    read_aT(o + E)
                    dve.wait_ge(comb_done, o + E + 1)

            dve.wait_ge(comb_done, E)
            for n in range(NT):
                dve.tensor_tensor(xt[:, n, :].rearrange("p (h q) -> p h q", h=2), ps[:, 4 + 2 * n:6 + 2 * n, :],
                                  xt[:, n, :].rearrange("p (h q) -> p h q", h=2), ALU.add).then_inc(x2_ready, 1)
            dve.wait_ge(gfin_ready, 1)
            for n in range(NT):
                norm(n, 4 + n)
                dve.scalar_tensor_tensor(out=xs[:, n, :], in0=xt[:, n, :], scalar=rstd[:, 4 + n:5 + n], in1=gfin,
                                         op0=ALU.mult, op1=ALU.mult).then_inc(fin_ready, 1)


_INS = ['x', 'attn_norm_g', 'w_in', 'cmp_pe_k', 'cmp_pe_v', 'cmp_w1_k', 'cmp_w2_k', 'cmp_w1_v', 'cmp_w2_v', 'w_out',
        'ffn_norm_g', 'w_router', 'b_router', 'w_up', 'b_up', 'w_down', 'b_down', 'final_norm_g']


def kernel(**inputs):
    import numpy as _np
    import concourse.bacc as _bacc
    from concourse import mybir as _mybir
    from concourse.bass_utils import run_bass_kernel_spmd as _run

    nc = _bacc.Bacc("TRN2", target_bir_lowering=False, num_devices=1)
    arrays, args = {}, []
    for name in _INS:
        a = _np.ascontiguousarray(inputs[name])
        arrays[f"in_{name}_dram"] = a
        args.append(nc.dram_tensor(f"in_{name}_dram", a.shape, _mybir.dt.from_np(a.dtype), kind="ExternalInput").ap())
    shape = arrays["in_x_dram"].shape
    args.append(nc.dram_tensor("out_0_dram", shape, _mybir.dt.float32, kind="ExternalOutput").ap())
    hybrid_layer(nc, *args)
    r = _run(nc, [arrays], core_ids=[0])
    return r.results[0]["out_0_dram"]
```

```python
from contextlib import ExitStack

import concourse.bass as bass
from concourse import mybir

P = 128
ALU = mybir.AluOpType
ACT = mybir.ActivationFunctionType
AX = mybir.AxisListType
F32 = mybir.dt.float32
I32 = mybir.dt.int32
U32 = mybir.dt.uint32
ds = bass.ds

TOK = 64
CAP = 64
BIG = 1e33
EPS = 1e-5


def hybrid_layer(nc, x, attn_norm_g, w_in, cmp_pe_k, cmp_pe_v, cmp_w1_k, cmp_w2_k, cmp_w1_v, cmp_w2_v, w_out,
                 ffn_norm_g, w_router, b_router, w_up, b_up, w_down, b_down, final_norm_g, out):
    _, S, D = x.shape
    E = w_router.shape[2]
    F = w_down.shape[2]
    HD = 64
    H = 8
    G = 2
    HG = H // G
    NT = S // P
    KD = D // P
    NC = (S - 32) // 16 + 1
    CMP_L = 32
    LP = CMP_L // 2
    TOPK = 4
    IN = w_in.shape[2]
    assert NT == 2 and KD == 8 and D == 1024 and F == 1024 and E == 32 and IN == 2840

    moba_slope = [2.0 ** (-8.0 * (2 * h + 1) / 16) for h in range(H)]
    nsa_slope = [2.0 ** (-8.0 * (2 * h + 2) / 16) for h in range(H)]
    nsa_order = [g * HG + j for j in range(HG) for g in range(G)]

    MORE = -(-S // CAP) - 1
    NOV = S * TOPK // (CAP + 1)

    CHUNK = 512
    chunk_width = [min(CHUNK, IN - c * CHUNK) for c in range(-(-IN // CHUNK))]
    UNITS = 16
    UNIT = 2048
    UP_UNITS = 8
    DOWN_UNITS = 4

    slots = [("moba", h) for h in range(H)] + [("slc", h) for h in nsa_order] + [("win", h) for h in nsa_order]
    NSLOT = len(slots)
    T_LAG, PV_LAG = 2, 3
    ZB = 4
    pre_jobs = ["mq0", "mk0", "mk1"]
    jobs_of_slot = {0: ["mq1"], 1: ["mv0"], 2: ["mv1"], 3: ["kcvc"], 4: ["ksvs"], 5: ["nq0"], 6: ["kwvw"],
                    7: ["vw1", "cm1"], 8: ["nq1"], 10: ["cm2"], 11: ["cs"], 12: ["ot0", "ot1"], 13: ["om00"],
                    14: ["om01"], 15: ["ct"], 16: ["om10"], 18: ["om11"]}
    jobs = pre_jobs + [n for s in sorted(jobs_of_slot) for n in jobs_of_slot[s]]
    job_at = {n: i for i, n in enumerate(jobs)}
    last_job_of_chunk = {0: "mq1", 1: "mk1", 2: "mv1", 3: "nq1", 4: "ksvs", 5: "vw1"}
    CZ_SLOT = 13

    ctx = ExitStack()
    with ctx:
        def sb(name, shape, dt=F32):
            return ctx.enter_context(nc.sbuf_tensor(name, shape, dt))

        def sem(name):
            return ctx.enter_context(nc.semaphore(name))

        ps = ctx.enter_context(nc.psum_tensor("ps", [P, 8, 512], F32))

        ring = sb("ring", [P, UNITS, UNIT])
        wout = ring[:, 12:16, :].rearrange("p u (k d) -> p (u k) d", k=2)
        xt = sb("xt", [P, NT, D])
        xs = sb("xs", [P, NT, D])
        xT = sb("xT", [P, KD, S])
        ident = sb("ident", [P, P])
        upper = sb("upper", [P, P])
        ones = sb("ones", [P, P])
        prm = sb("prm", [48, P])
        prmT = sb("prmT", [P, 48])
        w2k = sb("w2k", [HD, HD])
        w2v = sb("w2v", [HD, HD])
        wr = sb("wr", [P, KD, E])
        br = sb("br", [P, E])
        sq_sum = sb("sq_sum", [P, 6, 2])
        ms = sb("ms", [P, 6])
        root = sb("root", [P, 6])
        rstd = sb("rstd", [P, 6])
        w1k = wout[:, 0, :].rearrange("p (c j) -> p c j", j=HD)
        w1v = wout[:, 1, :].rearrange("p (c j) -> p c j", j=HD)
        gaT = prmT[:, 0:KD]
        gfT = prmT[:, KD:2 * KD]
        peT = [prmT[:, 16:32], prmT[:, 32:48]]

        WORK = 13280
        work = sb("work", [P, WORK])
        at = [0]

        def carve(n, *dims):
            a = work[:, at[0]:at[0] + n]
            at[0] += n
            assert at[0] <= WORK
            if len(dims) == 2:
                return a.rearrange("p (a b) -> p a b", a=dims[0])
            if len(dims) == 3:
                return a.rearrange("p (a b c) -> p a b c", a=dims[0], b=dims[1])
            return a

        mqT = carve(1024, 4, 256)
        mkT = carve(1024, 4, 256)
        nqT = carve(1024, 4, 256)
        ksT = carve(256)
        kwT = carve(256)
        mv = carve(1024, 2, 512)
        vs = carve(256, 2, 128)
        vw = carve(256, 2, 128)
        gates = carve(48, 2, 24)
        gtmp = carve(48, 2, 24)
        tabs = carve(8 * 256, 8, 256)
        dist = carve(256)
        z = carve(ZB * 384, ZB, 384)
        pT = carve(2 * 384, 2, 384)
        zmin = carve(2 * ZB, ZB, 2)
        zsum = carve(2 * ZB, ZB, 2)
        zrec = carve(2 * ZB, ZB, 2)
        R = [carve(2 * LP * 15, 2, LP, 15) for _ in range(2)]
        hx = carve(64)
        hsq = carve(64)
        ht = carve(64)
        hTk = carve(32)
        hTv = carve(2 * 128, 2, 4, 32)
        kcT = carve(32)
        vc = carve(2 * 256, 2, 256)
        cdist = carve(32, 2, 16)
        cmask = carve(32, 2, 16)
        ctab = carve(2 * 8 * 16, 2, 8, 16)
        cz = carve(2 * 8 * 32, 2, 8, 32)
        cmin = carve(16, 2, 8)
        csum = carve(16, 2, 8)
        crec = carve(16, 2, 8)
        pcT = carve(4 * 128, 4, 128)
        at[0] = 0
        iota_e = carve(32)
        iota_t = carve(128)
        lg = carve(64, 2, 32)
        top = carve(16, 2, 8)
        topi = carve(16, 2, 8).bitcast(U32)
        topf = carve(8, 2, 4)
        hot = carve(8 * 32, 2, 4, 32)
        hotw = carve(8 * 32, 2, 4, 32)
        tdiff = carve(8, 2, 4)
        texp = carve(8, 2, 4)
        tsum = carve(2)
        trec = carve(2)
        tw = carve(8, 2, 4)
        M = carve(64, 2, 32)
        posp = carve(66, 2, 33)
        Wt = carve(66, 2, 33)
        WT = carve(256)
        bd = carve(1024)
        gfin = carve(1024)
        brow = carve(2048)
        pcol = carve(2)
        pm = carve(128, 2, 64)
        pw = carve(256, 2, 128)
        xg = carve(512)
        xgT = carve(512, 8, 64)
        t1 = carve(512, 2, 256)
        t2 = carve(512, 2, 256)
        t3 = carve(512, 2, 256)
        av = carve(512, 2, 256)
        aT = carve(512, 4, 128)
        yv = carve(512)
        cT = carve(256, 2, 128)
        cnt = carve(1)
        ecol = carve(1)
        more_k = carve(MORE)
        flag = carve(MORE)
        nflag = carve(1)
        rank = carve(MORE)
        iota_o = carve(NOV)
        Rsel = carve(MORE * NOV, MORE, NOV)
        Rk = carve(NOV)
        Re = carve(NOV)
        Rb = carve(NOV)
        ovt = carve(2 * NOV + 1)
        ovi = carve(2 * NOV + 1).bitcast(I32)

        PJ = [0, 1]
        SB = [2, 3]
        TB = [4, 5]
        OB = [6, 7]
        XG, XTB = 0, 1
        UP = ps[:, 2:4, :]
        OUT = [[4, 5], [6, 7]]

        x_in = [sem(f"x_in{n}") for n in range(NT)]
        unit_in = [sem(f"unit_in{u}") for u in range(UNITS)]
        prm_in = sem("prm_in")
        cmpw_in = sem("cmpw_in")
        over_in = [sem(f"over_in{u}") for u in range(12)]
        router_in = sem("router_in")
        late_in = sem("late_in")
        brow_in = sem("brow_in")
        out_sent = sem("out_sent")
        ident_ready = sem("ident_ready")
        const_ready = sem("const_ready")
        pool_chain = sem("pool_chain")
        dist_ready = sem("dist_ready")
        tab_ready = sem("tab_ready")
        ctab_ready = sem("ctab_ready")
        iotas_ready = sem("iotas_ready")
        gfin_ready = sem("gfin_ready")
        prmT_ps = sem("prmT_ps")
        prmT_ready = sem("prmT_ready")
        squared = [sem(f"squared{h}") for h in range(2)]
        rooted = sem("rooted")
        dve_chain = sem("dve_chain")
        ms_ready = sem("ms_ready")
        rstd_ready = sem("rstd_ready")
        half_added = sem("half_added")
        xs_ready = [sem(f"xs_ready{h}") for h in range(2)]
        xT_ps = sem("xT_ps")
        xT_ready = sem("xT_ready")
        job_done = sem("job_done")
        bank_read = [sem(f"bank_read{b}") for b in range(2)]
        r_ready = sem("r_ready")
        gate_exp = sem("gate_exp")
        gates_ready = sem("gates_ready")
        s_done = sem("s_done")
        z_done = sem("z_done")
        exp_done = sem("exp_done")
        p_scaled = sem("p_scaled")
        pT_done = sem("pT_done")
        pT_read = sem("pT_read")
        pv_done = sem("pv_done")
        o_read = sem("o_read")
        gelu_t = sem("gelu_t")
        gelu_exp = sem("gelu_exp")
        gelu_done = sem("gelu_done")
        cz_ready = sem("cz_ready")
        cexp_done = sem("cexp_done")
        cp_ready = sem("cp_ready")
        half_done = sem("half_done")
        proj_done = sem("proj_done")
        cnt_done = sem("cnt_done")
        logits_done = sem("logits_done")
        td_ready = sem("td_ready")
        te_ready = sem("te_ready")
        m_ready = sem("m_ready")
        pos_done = sem("pos_done")
        w_ready = sem("w_ready")
        wT_done = sem("wT_done")
        wT_read = sem("wT_read")
        nflag_ready = sem("nflag_ready")
        rank_done = sem("rank_done")
        rsel_ready = sem("rsel_ready")
        ovt_done = sem("ovt_done")
        ovi_ready = sem("ovi_ready")
        pcol_ready = sem("pcol_ready")
        pm_ready = sem("pm_ready")
        pw_ready = sem("pw_ready")
        xg_done = sem("xg_done")
        xg_read = sem("xg_read")
        xgT_done = sem("xgT_done")
        xgT_read = sem("xgT_read")
        bias_used = sem("bias_used")
        up_used = sem("up_used")
        swi = sem("swi")
        sig_done = sem("sig_done")
        a_ready = sem("a_ready")
        aT_done = sem("aT_done")
        aT_read = sem("aT_read")
        down_used = sem("down_used")
        y_read = sem("y_read")
        cT_done = sem("cT_done")
        cT_read = sem("cT_read")
        comb_done = sem("comb_done")
        half_summed = sem("half_summed")
        fin_ready = sem("fin_ready")

        x_v = x.rearrange("o (n p) d -> (o n) p d", p=P)
        out_v = out.rearrange("o (n p) d -> (o n) p d", p=P)
        win_v = w_in.rearrange("o (k p) n -> p (o k) n", p=P)
        wout_v = w_out.rearrange("o (k p) n -> p (o k) n", p=P)
        up_v = w_up.rearrange("o e (k p) f -> (o e) k p f", p=P)
        down_v = w_down.rearrange("o e (u j p) d -> (o e) u p j d", j=2, p=P)
        bup_v = b_up.rearrange("o e f -> (o e) f")

        def win_unit(c, k):
            w = chunk_width[c]
            return ring[:, 2 * c + k // 4, (k % 4) * w:(k % 4) * w + w]

        def cmp_tokens(src, parity):
            return bass.AP(tensor=src.tensor, offset=src.offset + parity, ap=[list(src.ap[0]), [2, LP], [16, NC]])

        def head_of(slot):
            kind, h = slots[slot]
            if kind == "moba":
                b = (h % 2) * HD
                return (mqT[b:b + HD, h // 2, :], mkT[b:b + HD, h // 2, :],
                        lambda t: mv[:, t, h * HD:(h + 1) * HD], h * HD)
            g, j = h // HG, h % HG
            b = g * HD
            kT, v = (ksT, vs) if kind == "slc" else (kwT, vw)
            return nqT[b:b + HD, j, :], kT[b:b + HD, :], lambda t: v[:, t, b:b + HD], h * HD

        def job_free(eng, name):
            j = job_at[name]
            if j >= 2:
                eng.wait_ge(bank_read[j % 2], j // 2)

        def wait_job_read(eng, *names):
            for n in names:
                eng.wait_ge(bank_read[job_at[n] % 2], job_at[n] // 2 + 1)

        def job_bank(name):
            return ps[:, PJ[job_at[name] % 2], :]

        def unit_at(c, u):
            return (12 * c + u) % UNITS

        def unit_loaded(b4, c, u):
            return b4 * 48 + 16 * ((12 * c + u) // UNITS + 2)

        block = ctx.enter_context(nc.Block())

        @block.sync
        def _(sp):
            sp.dma_start(xt[:, 0, :], x_v[0]).then_inc(x_in[0], 16)
            sp.dma_start(prm[0:8, :], attn_norm_g.rearrange("o (k p) -> (o k) p", p=P)).then_inc(prm_in, 16)
            sp.dma_start(prm[8:16, :], ffn_norm_g.rearrange("o (k p) -> (o k) p", p=P)).then_inc(prm_in, 16)
            sp.dma_start(xt[:, 1, :], x_v[1]).then_inc(x_in[1], 16)
            sp.dma_start(prm[16:32, :], cmp_pe_k.rearrange("o (l t) d -> (o l) (t d)", t=2)).then_inc(prm_in, 16)
            sp.dma_start(prm[32:48, :], cmp_pe_v.rearrange("o (l t) d -> (o l) (t d)", t=2)).then_inc(prm_in, 16)
            for c in (0, 1, 2, 4, 3, 5):
                if c == 3:
                    sp.dma_start(w1k, cmp_w1_k.rearrange("o (c p) j -> p (o c) j", p=P)).then_inc(cmpw_in, 16)
                    sp.dma_start(w1v, cmp_w1_v.rearrange("o (c p) j -> p (o c) j", p=P)).then_inc(cmpw_in, 16)
                    sp.dma_start(w2k[:], cmp_w2_k[0]).then_inc(cmpw_in, 16)
                    sp.dma_start(w2v[:], cmp_w2_v[0]).then_inc(cmpw_in, 16)
                w = chunk_width[c]
                for half in range(2):
                    sp.dma_start(ring[:, 2 * c + half, 0:4 * w].rearrange("p (k n) -> p k n", k=4),
                                 win_v[:, 4 * half:4 * half + 4, c * CHUNK:c * CHUNK + w])\
                      .then_inc(unit_in[2 * c + half], 16)

            def load_wout(n):
                sp.dma_start(wout[:, 2 * n:2 * n + 2, :], wout_v[:, 2 * n:2 * n + 2, :]).then_inc(unit_in[12 + n], 16)

            def load_unit(e, u, slot, loaded):
                if u < UP_UNITS:
                    sp.dma_start(ring[:, slot, :], up_v[ds(e, 1), u].rearrange("a p f -> p (a f)"))\
                      .then_inc(loaded, 16)
                else:
                    sp.dma_start(ring[:, slot, :].rearrange("p (j d) -> p j d", j=2),
                                 down_v[ds(e, 1), u - UP_UNITS].rearrange("a p j d -> p (a j) d"))\
                      .then_inc(loaded, 16)

            sp.dma_start(wr[:], w_router.rearrange("o (k p) e -> p (o k) e", p=P)).then_inc(router_in, 16)
            sp.dma_start(br[:], b_router[0:1, :].partition_broadcast(P).rearrange("p o e -> p (o e)"))\
              .then_inc(router_in, 16)
            for n in range(1, 4):
                load_wout(n)
            for c in (0, 2, 1, 4, 5, 3):
                if c == 3:
                    sp.wait_ge(job_done, job_at["cm1"] + 1)
                    load_wout(0)
                sp.wait_ge(job_done, job_at[last_job_of_chunk[c]] + 1)
                for u in (2 * c, 2 * c + 1):
                    load_unit(0, u, u, unit_in[u])

            def load_block(b, c, e, first=False):
                for u in range(12):
                    if u < 4:
                        if first:
                            sp.wait_ge(proj_done, NT)
                        else:
                            sp.wait_ge(down_used, b * DOWN_UNITS + (u + 1 - 2 * DOWN_UNITS))
                    else:
                        sp.wait_ge(up_used, b * UP_UNITS + (u - 3 - UP_UNITS))
                    load_unit(e, u, unit_at(c, u), unit_in[unit_at(c, u)])

            load_block(1, 1, 1, first=True)
            load_block(2, 2, 2)
            with sp.Fori(0, (E - 4) // 4) as m:
                for r in range(4):
                    load_block(m * 4 + (3 + r), (3 + r) % 4, m * 4 + (3 + r))
            load_block(E - 1, 3, E - 1)
            sp.wait_ge(ovi_ready, 1)
            more = sp.value_load(ovi[0:1, 2 * NOV:2 * NOV + 1], min_val=0, max_val=NOV)
            with sp.If(more > 0):
                with sp.Fori(0, more) as o:
                    e = sp.value_load(ovi[0:1, ds(o, 1)], min_val=0, max_val=E - 1)
                    sp.wait_ge(down_used, o * DOWN_UNITS + E * DOWN_UNITS)
                    for u in range(12):
                        load_unit(e, u, u, over_in[u])
            for n in range(NT):
                for half in range(2):
                    h = slice(512 * half, 512 * half + 512)
                    sp.wait_ge(fin_ready, 2 * n + half + 1)
                    sp.dma_start(out_v[n][:, h], xs[:, n, h]).then_inc(out_sent, 16)
            sp.wait_ge(out_sent, 32 * NT)

        @block.gpsimd
        def _(pool):
            chain = [0]

            def link(ins):
                chain[0] += 1
                ins.then_inc(pool_chain, 1)
                pool.wait_ge(pool_chain, chain[0])

            link(pool.memset(ident[:], 0.0))
            pool.affine_select(out=ident[:], in_=ident[:], compare_op=ALU.not_equal, fill=1.0, base=0,
                               pattern=[[-1, P]], channel_multiplier=1).then_inc(ident_ready, 1)
            link(pool.iota(dist, pattern=[[-1, 2 * P]], base=P, channel_multiplier=1,
                           allow_small_or_imprecise_dtypes=True))
            pool.affine_select(out=dist, in_=dist, compare_op=ALU.is_ge, fill=BIG, base=P,
                               pattern=[[-1, 2 * P]], channel_multiplier=1).then_inc(dist_ready, 1)
            pool.wait_ge(dist_ready, 1)
            for h in range(H):
                pool.tensor_scalar(tabs[:, h, :], dist, moba_slope[h], None, ALU.mult).then_inc(tab_ready, 1)
            pool.memset(ones[:], 1.0).then_inc(const_ready, 1)
            pool.memset(upper[:], 1.0).then_inc(const_ready, 1)
            pool.memset(cz, 0.0).then_inc(const_ready, 1)
            pool.memset(hTv[0:HD], 0.0).then_inc(const_ready, 1)
            pool.memset(vc, 0.0).then_inc(const_ready, 1)
            pool.memset(kcT, 0.0).then_inc(const_ready, 1)
            pool.wait_ge(const_ready, 6)
            pool.affine_select(out=upper[:], in_=upper[:], compare_op=ALU.is_gt, fill=0.0, base=0,
                               pattern=[[1, P]], channel_multiplier=-1).then_inc(const_ready, 1)
            link(pool.iota(cdist, pattern=[[P, NT], [-16, 16]], base=-(CMP_L - 1), channel_multiplier=1,
                           allow_small_or_imprecise_dtypes=True))
            link(pool.tensor_scalar(cmask, cdist, 0.0, None, ALU.is_ge))
            link(pool.affine_select(out=cdist, in_=cdist, compare_op=ALU.is_ge, fill=BIG, base=-(CMP_L - 1),
                                    pattern=[[P, NT], [-16, 16]], channel_multiplier=1))
            for h in range(H):
                pool.tensor_scalar(ctab[:, :, h, :], cdist, nsa_slope[h], None, ALU.mult).then_inc(ctab_ready, 1)
            for n, h in enumerate(nsa_order):
                pool.wait_ge(z_done, n + 1)
                pool.tensor_scalar(tabs[:, n, :], dist, nsa_slope[h], None, ALU.mult).then_inc(tab_ready, 1)
            pool.wait_ge(proj_done, NT)
            pool.iota(iota_e, pattern=[[1, E]], base=0, channel_multiplier=0,
                      allow_small_or_imprecise_dtypes=True).then_inc(iotas_ready, 1)
            pool.iota(iota_t, pattern=[[0, 2], [1, TOK]], base=1, channel_multiplier=0,
                      allow_small_or_imprecise_dtypes=True).then_inc(iotas_ready, 1)
            pool.iota(iota_o, pattern=[[1, NOV]], base=0, channel_multiplier=0,
                      allow_small_or_imprecise_dtypes=True).then_inc(iotas_ready, 1)
            pool.iota(more_k, pattern=[[CAP, MORE]], base=CAP, channel_multiplier=0,
                      allow_small_or_imprecise_dtypes=True).then_inc(iotas_ready, 1)
            pool.iota(ecol, pattern=[[0, 1]], base=0, channel_multiplier=1,
                      allow_small_or_imprecise_dtypes=True).then_inc(iotas_ready, 1)
            pool.memset(posp, 0.0).then_inc(iotas_ready, 1)
            pool.memset(Wt, 0.0).then_inc(iotas_ready, 1)
            pool.wait_ge(late_in, 32)
            pool.partition_broadcast(gfin, gfin[0:1, :], P).then_inc(gfin_ready, 1)
            if CAP < 64:
                pool.wait_ge(iotas_ready, 7)
                pool.memset(iota_t[:, CAP:64], -1000.0).then_inc(iotas_ready, 1)
                pool.memset(iota_t[:, 64 + CAP:128], -1000.0).then_inc(iotas_ready, 1)
        IOTAS = 7 if CAP == 64 else 9

        @block.scalar
        def _(act):
            act.wait_ge(ident_ready, 1)
            act.activation(root[:, 5:6], ident[:, 0:1], ACT.Sqrt)

            def square(n, j):
                act.activation(xs[:, n, 0:512], xt[:, n, 0:512], ACT.Square, accum_out=sq_sum[:, j, 0:1])\
                   .then_inc(squared[0], 1)

            def scale(n, j):
                act.wait_ge(ms_ready, j + 1)
                act.activation(root[:, j:j + 1], ms[:, j:j + 1], ACT.Sqrt).then_inc(rooted, 1)
                act.wait_ge(rstd_ready, j + 1)
                if j < 4:
                    act.activation(xs[:, n, 0:512], xt[:, n, 0:512], ACT.Copy, scale=rstd[:, j:j + 1])\
                       .then_inc(xs_ready[0], 1)

            for n in range(NT):
                act.wait_ge(x_in[n], 16)
                square(n, n)
                scale(n, n)

            def read_job(name):
                j = job_at[name]
                act.wait_ge(job_done, j + 1)
                b = job_bank(name)
                pair = b.rearrange("p (a q) -> p a q", a=2)
                kind, n = name[:2], int(name[2]) if name[2:3].isdigit() else 0
                if kind in ("mq", "nq"):
                    t = act.activation((mqT if kind == "mq" else nqT)[:, 2 * n:2 * n + 2, :], pair, ACT.Copy,
                                       scale=-HD ** -0.5)
                elif kind == "mk":
                    t = act.activation(mkT[:, 2 * n:2 * n + 2, :], pair, ACT.Copy)
                elif kind == "mv":
                    t = act.activation(mv[:, n, :], b, ACT.Copy)
                elif kind == "ks":
                    act.activation(ksT, b[:, 0:256], ACT.Copy)
                    t = act.activation(vs, b[:, 256:512].rearrange("p (t n) -> p t n", t=2), ACT.Copy)
                elif kind == "kw":
                    act.activation(kwT, b[:, 0:256], ACT.Copy)
                    act.activation(vw[:, 0, :], b[:, 256:384], ACT.Copy)
                    t = act.activation(gtmp[:, 0, :], b[:, 384:408], ACT.Exp, scale=-1.0)
                elif kind == "vw":
                    act.activation(vw[:, 1, :], b[:, 0:128], ACT.Copy)
                    t = act.activation(gtmp[:, 1, :], b[:, 128:152], ACT.Exp, scale=-1.0)
                elif kind == "cm":
                    act.wait_ge(const_ready, 7)
                    for g in range(G):
                        k = slice(g * HD, (g + 1) * HD)
                        act.activation(kcT[k, 16 * g:16 * g + NC], b[k, 0:NC], ACT.Copy)
                    for a in range(HG):
                        k = slice(32 * a, 32 * a + 32)
                        t = act.activation(vc[k, :, a * HD:(a + 1) * HD],
                                           b[k, 64:192].rearrange("p (g d) -> p g d", g=2), ACT.Copy)
                elif kind == "ot":
                    t = act.activation(xT[:, 0:4, n * P:(n + 1) * P], b.rearrange("p (k q) -> p k q", k=4), ACT.Copy)
                elif kind == "ct":
                    t = act.activation(pcT, b.rearrange("p (a q) -> p a q", a=4), ACT.Copy)
                t.then_inc(bank_read[j % 2], 1)

            by_act = [n for n in jobs if n not in ("kcvc", "cm1", "cs", "om00", "om01", "om10", "om11")]
            for name in pre_jobs:
                read_job(name)
            for s in range(NSLOT + PV_LAG + 1):
                if s >= T_LAG and s - T_LAG < NSLOT:
                    n = s - T_LAG
                    act.wait_ge(pT_done, n + 1)
                    if n >= 2:
                        act.wait_ge(pv_done, n - 1)
                    act.activation(pT[:, n % 2, :], ps[:, TB[n % 2], 0:384], ACT.Copy).then_inc(pT_read, 1)
                if s < NSLOT:
                    act.wait_ge(z_done, s + 1)
                    zb = z[:, s % ZB, :]
                    act.activation(zb[:, 0:128], zb[:, 0:128], ACT.Exp, bias=zmin[:, s % ZB, 0:1], scale=-1.0,
                                   accum_out=zsum[:, s % ZB, 0:1])
                    act.activation(zb[:, 128:384], zb[:, 128:384], ACT.Exp, bias=zmin[:, s % ZB, 1:2], scale=-1.0,
                                   accum_out=zsum[:, s % ZB, 1:2]).then_inc(exp_done, 1)
                for name in jobs_of_slot.get(s, []):
                    if name in by_act:
                        read_job(name)
                    if name == "cm1":
                        act.wait_ge(gelu_t, 1)
                        act.activation(hsq[0:HD, 0:62], ht[0:HD, 0:62], ACT.Exp, scale=-2.0 * 0.7978845608028654)\
                           .then_inc(gelu_exp, 1)
                    if name == "cs":
                        act.wait_ge(cz_ready, 1)
                        act.activation(cz[:, :, :, 0:NC], cz[:, :, :, 0:NC], ACT.Exp, scale=-1.0)\
                           .then_inc(cexp_done, 1)

            for n in range(NT):
                act.wait_ge(xT_ps, 4 + n + 1)
                act.activation(xT[:, 4:8, n * P:(n + 1) * P], ps[:, PJ[n], :].rearrange("p (k q) -> p k q", k=4),
                               ACT.Copy).then_inc(xT_ready, 1)

            act.wait_ge(pv_done, NSLOT + NT)
            act.dma_start(brow[0:1, :], bup_v[0:1, :]).then_inc(brow_in, 16)
            act.dma_start(bd[0:E, :], b_down[0]).then_inc(late_in, 16)
            act.dma_start(gfin[0:1, :], final_norm_g.rearrange("(o d) -> o d", o=1)).then_inc(late_in, 16)
            for n in range(NT):
                act.wait_ge(half_added, 2 * n + 1)
                square(n, 2 + n)
                scale(n, 2 + n)
            act.wait_ge(td_ready, 1)
            act.activation(texp, tdiff, ACT.Exp).then_inc(te_ready, 1)

            def read_xg(b):
                act.wait_ge(xg_done, b + 1)
                act.activation(xg, ps[:, XG, :], ACT.Copy).then_inc(xg_read, 1)

            def sigmoid(b):
                act.wait_ge(swi, b * 3 + 1)
                act.activation(t2, t1, ACT.Sigmoid, scale=1.702).then_inc(sig_done, 1)

            def read_rest(b, prev):
                act.wait_ge(cT_done, b + 1)
                if prev:
                    act.wait_ge(comb_done, b)
                act.activation(cT, ps[:, XG, 0:256].rearrange("p (n q) -> p n q", n=2), ACT.Copy).then_inc(cT_read, 1)
                act.wait_ge(aT_done, b + 1)
                act.activation(aT[:, 0:2, :], UP[:, 0, 0:256].rearrange("p (a q) -> p a q", a=2), ACT.Copy)\
                   .then_inc(aT_read, 1)
                act.wait_ge(down_used, b * DOWN_UNITS + DOWN_UNITS)
                act.activation(yv, ps[:, XG, :], ACT.Copy).then_inc(y_read, 1)

            def load_brow(b, e):
                act.wait_ge(bias_used, b)
                act.dma_start(brow[0:1, :], bup_v[ds(e, 1), :]).then_inc(brow_in, 16)

            read_xg(0)
            load_brow(1, 1)
            act.wait_ge(wT_done, 1)
            act.activation(WT[0:E, :], ps[0:E, OUT[0][1], 128:384], ACT.Copy).then_inc(wT_read, 1)
            sigmoid(0)
            read_xg(1)
            read_rest(0, False)
            with act.Fori(1, E - 1) as i:
                load_brow(i + 1, i + 1)
                sigmoid(i)
                read_xg(i + 1)
                read_rest(i, True)
            sigmoid(E - 1)
            read_rest(E - 1, True)
            act.wait_ge(ovi_ready, 1)
            more = act.value_load(ovi[0:1, 2 * NOV:2 * NOV + 1], min_val=0, max_val=NOV)
            with act.If(more > 0):
                with act.Fori(0, more) as o:
                    e = act.value_load(ovi[0:1, ds(o, 1)], min_val=0, max_val=E - 1)
                    load_brow(o + E, e)
                    read_xg(o + E)
                    sigmoid(o + E)
                    read_rest(o + E, True)

            act.activation(root[:, 5:6], ident[:, 0:1], ACT.Sqrt)
            for n in range(NT):
                act.wait_ge(half_added, 4 + 2 * n + 1)
                square(n, 4 + n)
                scale(n, 4 + n)

        @block.tensor
        def _(pe):
            pe.wait_ge(ident_ready, 1)
            pe.wait_ge(prm_in, 64)
            pe.transpose(ps[:, PJ[0], 0:48], prm[:, :], ident[0:48, 0:48]).then_inc(prmT_ps, 1)

            def transposes(n, k0, bank):
                for k in range(4):
                    t = pe.transpose(ps[:, bank, k * P:(k + 1) * P], xs[:, n, (k0 + k) * P:(k0 + k + 1) * P],
                                     ident[:, :])
                t.then_inc(xT_ps, 1)

            for n in range(NT):
                for half in range(2):
                    pe.wait_ge(xs_ready[half], n + 1)
                    b = 2 * n + half
                    if b == 0:
                        pe.wait_ge(prmT_ready, 1)
                    if b >= 2:
                        pe.wait_ge(xT_ready, b - 1)
                    transposes(n, 4 * half, PJ[half])
            pe.wait_ge(xT_ready, 4)

            def across(dst, c, lhs):
                for k in range(KD):
                    pe.wait_ge(unit_in[2 * c + k // 4], 16)
                    t = pe.matmul(dst, lhs(win_unit(c, k)), xT[:, k, :], start=(k == 0), stop=(k == KD - 1))
                return t

            def along(dst, c, n, lo, hi):
                for k in range(KD):
                    pe.wait_ge(unit_in[2 * c + k // 4], 16)
                    t = pe.matmul(dst, xT[:, k, n * P:(n + 1) * P], win_unit(c, k)[:, lo:hi],
                                  start=(k == 0), stop=(k == KD - 1))
                return t

            def job(name):
                j = job_at[name]
                job_free(pe, name)
                b = job_bank(name)
                kind = name[:2]
                if kind in ("mq", "mk"):
                    for a in range(2):
                        o = (2 * int(name[2]) + a) * P
                        t = across(b[:, a * S:(a + 1) * S], 0 if kind == "mq" else 1, lambda w: w[:, o:o + P])
                elif kind == "mv":
                    t = along(b, 2, int(name[2]), 0, 512)
                elif kind == "nq":
                    for a in range(2):
                        o = (2 * int(name[2]) + a) * HD
                        for k in range(KD):
                            pe.wait_ge(unit_in[6 + k // 4], 16)
                            for g in range(G):
                                t = pe.matmul(b[g * HD:(g + 1) * HD, a * S:(a + 1) * S],
                                              win_unit(3, k)[:, g * S + o:g * S + o + HD], xT[:, k, :],
                                              start=(k == 0), stop=(k == KD - 1), skip_group_check=True)
                elif kind == "kc":
                    for a in range(2):
                        t = across(b[:, a * S:(a + 1) * S], 4, lambda w: w[:, a * P:(a + 1) * P])
                elif kind == "ks":
                    across(b[:, 0:S], 4, lambda w: w[:, 2 * P:3 * P])
                    for n in range(NT):
                        t = along(b[:, S + n * P:S + (n + 1) * P], 4, n, 3 * P, 4 * P)
                elif kind == "kw":
                    across(b[:, 0:S], 5, lambda w: w[:, 0:P])
                    t = along(b[:, S:S + 152], 5, 0, P, 280)
                elif kind == "vw":
                    t = along(b[:, 0:152], 5, 1, P, 280)
                elif name == "cm1":
                    pe.wait_ge(cmpw_in, 64)
                    pe.wait_ge(r_ready, 4)
                    for i, w in enumerate((w1k, w1v)):
                        for c in range(LP):
                            t = pe.matmul(b[0:HD, 32 * i:32 * i + 30], w[:, c, :], R[i][:, :, c, :],
                                          start=(c == 0), stop=(c == LP - 1))
                elif name == "cm2":
                    pe.wait_ge(gelu_done, 2)
                    for g in range(G):
                        pe.matmul(b[g * HD:(g + 1) * HD, 0:NC], w2k[:], hTk[0:HD, g * NC:(g + 1) * NC],
                                  start=True, stop=True)
                    for g in range(G):
                        t = pe.matmul(b[:, 64 + g * HD:64 + (g + 1) * HD],
                                      hTv[0:HD, g].rearrange("p a n -> p (a n)"), w2v[:], start=True, stop=True)
                elif kind == "cs":
                    wait_job_read(pe, "cm2", "nq0", "nq1")
                    for a in range(NT * HG):
                        n, q = a // HG, a % HG
                        t = pe.matmul(b[:, a * 32:(a + 1) * 32], nqT[:, q, n * P:(n + 1) * P], kcT,
                                      start=True, stop=True)
                elif kind == "ct":
                    pe.wait_ge(cp_ready, 1)
                    for a in range(4):
                        t = pe.transpose(b[:, a * P:(a + 1) * P],
                                         cz[:, a // 2, 4 * (a % 2):4 * (a % 2) + 4, :].rearrange("p h c -> p (h c)"),
                                         ident[:, :])
                elif kind == "ot":
                    n = int(name[2])
                    pe.wait_ge(o_read, 1)
                    for k in range(4):
                        t = pe.transpose(b[:, k * P:(k + 1) * P], xs[:, n, k * P:(k + 1) * P], ident[:, :])
                elif kind == "om":
                    n, half = int(name[2]), int(name[3])
                    wait_job_read(pe, "ot%d" % n)
                    t = project(b, n, half, 0)
                t.then_inc(job_done, 1)

            def project(dst, n, half, k0):
                for k in range(k0, k0 + 4):
                    pe.wait_ge(unit_in[12 + k // 2], 16)
                    t = pe.matmul(dst, xT[:, k, n * P:(n + 1) * P], wout[:, k, half * 512:(half + 1) * 512],
                                  start=(k == k0), stop=(k == k0 + 3))
                return t

            def scores(s):
                qT, kT, _, _ = head_of(s)
                kind, h = slots[s]
                if kind == "moba":
                    wait_job_read(pe, *(("mq0", "mk0") if h < 4 else ("mq1", "mk1")))
                else:
                    wait_job_read(pe, "nq0" if h % HG < 2 else "nq1", "ksvs" if kind == "slc" else "kwvw")
                if s >= 2:
                    pe.wait_ge(z_done, s - 1)
                b = ps[:, SB[s % 2], :]
                pe.matmul(b[:, 0:P], qT[:, 0:P], kT[:, 0:P], start=True, stop=True)
                pe.matmul(b[:, P:P + S], qT[:, P:S], kT, start=True, stop=True).then_inc(s_done, 1)

            def turn(s):
                pe.wait_ge(p_scaled, s + 1)
                if s >= 2:
                    pe.wait_ge(pT_read, s - 1)
                for k in range(3):
                    t = pe.transpose(ps[:, TB[s % 2], k * P:(k + 1) * P], z[:, s % ZB, (0, P, 2 * P)[k]:][:, 0:P],
                                     ident[:, :])
                t.then_inc(pT_done, 1)

            def values(s):
                _, _, v, o = head_of(s)
                wait_job_read(pe, *{"moba": ("mv0", "mv1"), "slc": ("ksvs",), "win": ("kwvw", "vw1")}[slots[s][0]])
                pe.wait_ge(pT_read, s + 1)
                if s == H:
                    pe.wait_ge(o_read, 1)
                first = s in (0, H)
                p = pT[:, s % 2, :]
                pe.matmul(ps[:, OB[0], o:o + HD], p[:, 0:P], v(0), start=first, stop=True, skip_group_check=True)
                pe.matmul(ps[:, OB[1], o:o + HD], p[:, P:2 * P], v(0), start=first, stop=False,
                          skip_group_check=True)
                pe.matmul(ps[:, OB[1], o:o + HD], p[:, 2 * P:3 * P], v(1), start=False, stop=True,
                          skip_group_check=True).then_inc(pv_done, 1)

            for name in pre_jobs:
                job(name)
            for s in range(NSLOT + PV_LAG + 1):
                if s < NSLOT:
                    scores(s)
                if s >= T_LAG and s - T_LAG < NSLOT:
                    turn(s - T_LAG)
                if s >= PV_LAG and s - PV_LAG < NSLOT:
                    values(s - PV_LAG)
                for name in jobs_of_slot.get(s, []):
                    job(name)
            wait_job_read(pe, "ct")
            for n in range(NT):
                for g in range(G):
                    t = pe.matmul(ps[:, OB[n], g * 256:(g + 1) * 256], pcT[:, 2 * n + g, :], vc[:, g, :],
                                  start=False, stop=True, skip_group_check=True)
                t.then_inc(pv_done, 1)

            for n in range(NT):
                pe.wait_ge(o_read, 2 + n)
                pe.wait_ge(bank_read[(len(jobs) - 2 + n) % 2], (len(jobs) - 2 + n) // 2 + 1)
                transposes(n, 4, PJ[n])
            for n in range(NT):
                pe.wait_ge(xT_ready, 4 + n + 1)
                for half in range(2):
                    t = project(ps[:, 2 + 2 * n + half, :], n, half, 4)
                    if half == 0:
                        t.then_inc(half_done, 1)
                t.then_inc(proj_done, 1)

            pe.wait_ge(router_in, 32)
            for n in range(NT):
                for half in range(2):
                    pe.wait_ge(xs_ready[half], NT + n + 1)
                    if n == 1:
                        pe.wait_ge(xT_ready, 6 + half + 1)
                    transposes(n, 4 * half, PJ[half])
                for k in range(KD):
                    if k % 4 == 0:
                        pe.wait_ge(xT_ready, 6 + 2 * n + k // 4 + 1)
                    t = pe.matmul(ps[:, OUT[1][0], n * E:(n + 1) * E], xT[:, k, n * P:(n + 1) * P], wr[:, k, :],
                                  start=(k == 0), stop=(k == KD - 1))
            t.then_inc(logits_done, 1)
            def gather(b, first=False):
                pe.wait_ge(pm_ready, b + 1)
                if not first:
                    pe.wait_ge(y_read, b - 1)
                for n in range(NT):
                    for h in range(2):
                        t = pe.matmul(ps[h * 64:(h + 1) * 64, XG, :], pm[:, n, :], xs[:, n, h * 512:(h + 1) * 512],
                                      start=(n == 0), stop=(n == 1), skip_group_check=True)
                t.then_inc(xg_done, 1)

            def gather_turn(b):
                pe.wait_ge(xg_read, b + 1)
                for j in range(4):
                    t = pe.transpose(ps[:, XTB, j * P:(j + 1) * P], xg[:, j * P:(j + 1) * P], ident[:, :])
                t.then_inc(xgT_done, 1)

            def up_bias(b, prev):
                pe.wait_ge(brow_in, b * 16 + 16)
                if prev:
                    pe.wait_ge(aT_read, b * 2)
                for c in range(4):
                    t = pe.matmul(UP[(c % 2) * 64:(c % 2) * 64 + 64, c // 2, :], ones[0:1, 0:64],
                                  brow[0:1, c * 512:(c + 1) * 512], start=True, stop=False, skip_group_check=True)
                t.then_inc(bias_used, 1)

            def up(b, prev, unit, biased=False):
                if not biased:
                    up_bias(b, prev)
                pe.wait_ge(xgT_read, b + 1)
                for k in range(KD):
                    slot = unit(k)
                    for c in range(4):
                        t = pe.matmul(UP[(c % 2) * 64:(c % 2) * 64 + 64, c // 2, :], xgT[:, k, :],
                                      ring[:, slot, c * 512:(c + 1) * 512], start=False, stop=(k == KD - 1),
                                      skip_group_check=True)
                    t.then_inc(up_used, 1)

            def combine_turn(b, ahead):
                pe.wait_ge(pw_ready, b + 1)
                pe.wait_ge(xg_read, b + 1 + ahead)
                for n in range(NT):
                    t = pe.transpose(ps[:, XG, n * P:(n + 1) * P], pw[:, n, :], ident[:, :])
                t.then_inc(cT_done, 1)

            def act_turn(b):
                pe.wait_ge(a_ready, b + 1)
                for j in range(4):
                    t = pe.transpose(UP[:, j // 2, (j % 2) * P:(j % 2 + 1) * P], av[:, j // 2, (j % 2) * P:(j % 2 + 1) * P],
                                     ident[:, :])
                t.then_inc(aT_done, 1)

            def down(b, unit):
                pe.wait_ge(aT_read, b * 2 + 2)
                pe.wait_ge(cT_read, b + 1)
                for u in range(DOWN_UNITS):
                    slot = unit(UP_UNITS + u)
                    for j in range(2):
                        for h in range(2):
                            t = pe.matmul(ps[h * 64:(h + 1) * 64, XG, :],
                                          aT[:, 2 * (u // 2) + j, (u % 2) * 64:(u % 2) * 64 + 64],
                                          ring[:, slot, j * D + h * 512:j * D + (h + 1) * 512],
                                          start=(u == 0 and j == 0), stop=(u == DOWN_UNITS - 1 and j == 1),
                                          skip_group_check=True)
                    t.then_inc(down_used, 1)

            def combine(b, last=False):
                pe.wait_ge(y_read, b + 1)
                for n in range(NT):
                    for h in range(2):
                        t = pe.matmul(ps[:, OUT[n][h], :], cT[h * 64:(h + 1) * 64, n, :], yv[h * 64:(h + 1) * 64, :],
                                      start=False, stop=True, skip_group_check=True)
                        if last and n == 0:
                            t.then_inc(half_summed, 1)
                t.then_inc(comb_done, 1)

            def in_ring(b4, c):
                def unit(u):
                    pe.wait_ge(unit_in[unit_at(c, u)], unit_loaded(b4, c, u))
                    return unit_at(c, u)
                return unit

            def run(b, b4, c):
                unit = in_ring(b4, c)
                up(b, True, unit)
                gather(b + 1)
                combine(b - 1)
                combine_turn(b, 1)
                gather_turn(b + 1)
                act_turn(b)
                down(b, unit)

            pe.wait_ge(half_added, 2 * NT)
            pe.wait_ge(const_ready, 7)
            up_bias(0, False)
            pe.wait_ge(m_ready, 1)
            pe.wait_ge(const_ready, 7)
            b = ps[:, OUT[1][1], :]
            pe.matmul(b[:, 0:E], upper[:], M[:, 0, :], start=True, stop=True)
            pe.matmul(b[:, E:2 * E], ones[:], M[:, 0, :], start=True, stop=False)
            pe.matmul(b[:, E:2 * E], upper[:], M[:, 1, :], start=False, stop=True).then_inc(pos_done, 1)
            gather(0, first=True)
            gather_turn(0)
            up(0, False, in_ring(0, 0), biased=True)
            gather(1, first=True)
            b = ps[:, OUT[1][1], :]
            for n in range(NT):
                t = pe.matmul(b[0:E, 64:65], M[:, n, :], ones[:, 0:1], start=(n == 0), stop=(n == 1))
            t.then_inc(cnt_done, 1)
            pe.wait_ge(w_ready, 1)
            for n in range(NT):
                t = pe.transpose(ps[0:E, OUT[0][1], P + n * P:P + (n + 1) * P], Wt[:, n, 0:E], ident[:, :])
            t.then_inc(wT_done, 1)
            combine_turn(0, 1)
            gather_turn(1)
            act_turn(0)
            down(0, in_ring(0, 0))
            pe.wait_ge(nflag_ready, 1)
            pe.matmul(ps[0:E, OUT[0][0], 0:1], upper[0:E, 0:E], nflag[0:E], start=True, stop=True)\
              .then_inc(rank_done, 1)
            up(1, True, in_ring(0, 1))
            pe.wait_ge(rsel_ready, 3)
            b = ps[:, OUT[0][0], :]
            pe.matmul(b[:, 64:64 + NOV], ones[0:E, :], Re[0:E, :], start=True, stop=True)
            pe.matmul(b[:, 64 + NOV:64 + 2 * NOV], ones[0:E, :], Rb[0:E, :], start=True, stop=True)
            pe.matmul(b[:, 64 + 2 * NOV:65 + 2 * NOV], ones[0:E, :], nflag[0:E], start=True, stop=True)\
              .then_inc(ovt_done, 1)
            gather(2)
            pe.wait_ge(wT_read, 1)
            pe.wait_ge(ovi_ready, 1)
            pe.wait_ge(late_in, 32)
            for n in range(NT):
                for h in range(2):
                    pe.matmul(ps[:, OUT[n][h], :], WT[0:E, n * P:(n + 1) * P], bd[0:E, h * 512:(h + 1) * 512],
                              start=True, stop=False, skip_group_check=True)
            combine(0)
            combine_turn(1, 1)
            gather_turn(2)
            act_turn(1)
            down(1, in_ring(0, 1))
            run(2, 0, 2)
            with pe.Fori(0, (E - 4) // 4) as m:
                for r in range(4):
                    run(m * 4 + (3 + r), m + (3 + r) // 4, (3 + r) % 4)
            last = in_ring(E // 4 - 1, 3)
            up(E - 1, True, last)
            combine(E - 2)
            combine_turn(E - 1, 0)
            act_turn(E - 1)
            down(E - 1, last)
            combine(E - 1, last=True)
            more = pe.value_load(ovi[0:1, 2 * NOV:2 * NOV + 1], min_val=0, max_val=NOV)
            with pe.If(more > 0):
                with pe.Fori(0, more) as o:
                    def over(u):
                        pe.wait_ge(over_in[u], o * 16 + 16)
                        return u

                    gather(o + E)
                    gather_turn(o + E)
                    up(o + E, True, over)
                    combine_turn(o + E, 0)
                    act_turn(o + E)
                    down(o + E, over)
                    combine(o + E)

        @block.vector
        def _(dve):
            chain = [0]

            def link(ins):
                chain[0] += 1
                ins.then_inc(dve_chain, 1)
                dve.wait_ge(dve_chain, chain[0])

            def square(n, j):
                dve.tensor_tensor_reduce(xs[:, n, 512:1024], xt[:, n, 512:1024], xt[:, n, 512:1024], 1.0, 0.0,
                                         ALU.mult, ALU.add, sq_sum[:, j, 1:2]).then_inc(squared[1], 1)

            def scale(n, j):
                for h in range(2):
                    dve.wait_ge(squared[h], j + 1)
                link(dve.tensor_tensor(ms[:, j:j + 1], sq_sum[:, j, 0:1], sq_sum[:, j, 1:2], ALU.add))
                dve.tensor_scalar(ms[:, j:j + 1], ms[:, j:j + 1], 1.0 / D, EPS, ALU.mult, ALU.add)\
                   .then_inc(ms_ready, 1)
                dve.wait_ge(rooted, j + 1)
                dve.reciprocal(rstd[:, j:j + 1], root[:, j:j + 1]).then_inc(rstd_ready, 1)
                dve.wait_ge(rstd_ready, j + 1)
                if j < 4:
                    dve.tensor_scalar(xs[:, n, 512:1024], xt[:, n, 512:1024], rstd[:, j:j + 1], None, ALU.mult)\
                       .then_inc(xs_ready[1], 1)

            def add(n, half, bank):
                h = slice(512 * half, 512 * half + 512)
                return dve.tensor_tensor(xt[:, n, h], ps[:, bank, :], xt[:, n, h], ALU.add)

            def read_xT(b, base, gain):
                n, half = b // 2, b % 2
                dve.wait_ge(xT_ps, base + b + 1)
                dve.tensor_tensor(xT[:, 4 * half:4 * half + 4, n * P:(n + 1) * P],
                                  ps[:, PJ[half], :].rearrange("p (k q) -> p k q", k=4),
                                  gain[:, 4 * half:4 * half + 4].unsqueeze(2).broadcast_to([P, 4, P]),
                                  ALU.mult).then_inc(xT_ready, 1)

            for n in range(NT):
                dve.wait_ge(x_in[n], 16)
                square(n, n)
                if n == 0:
                    scale(0, 0)
            dve.wait_ge(prmT_ps, 1)
            dve.tensor_copy(prmT[:, :], ps[:, PJ[0], 0:48]).then_inc(prmT_ready, 1)
            dve.wait_ge(prmT_ready, 1)
            scale(1, 1)
            for b in range(4):
                read_xT(b, 0, gaT)

            def scale_p(s):
                kind, h = slots[s]
                dve.wait_ge(exp_done, s + 1)
                q = s % ZB
                link(dve.tensor_scalar(zrec[:, q, :], zsum[:, q, :], 1e-30, None, ALU.max))
                link(dve.reciprocal(zrec[:, q, :], zrec[:, q, :]))
                for n, (a, b) in enumerate(((0, 128), (128, 384))):
                    gate = {"moba": None, "slc": 1, "win": 2}[kind]
                    zb = z[:, q, a:b]
                    if gate is None:
                        t = dve.tensor_scalar(zb, zb, zrec[:, q, n:n + 1], None, ALU.mult)
                    else:
                        c = 3 * h + gate
                        t = dve.tensor_scalar(zb, zb, zrec[:, q, n:n + 1], gates[:, n, c:c + 1], ALU.mult, ALU.mult)
                t.then_inc(p_scaled, 1)

            for s in range(NSLOT + PV_LAG + 1):
                if s < NSLOT:
                    q = s % ZB
                    dve.wait_ge(s_done, s + 1)
                    dve.wait_ge(tab_ready, s % H + 1 + (H if s >= H else 0))
                    if s >= ZB:
                        dve.wait_ge(pT_done, s - ZB + 1)
                    b = ps[:, SB[s % 2], :]
                    dve.tensor_tensor_reduce(z[:, q, 0:P], b[:, 0:P], tabs[:, s % H, P:2 * P], 1.0, 3e38,
                                             ALU.add, ALU.min, zmin[:, q, 0:1])
                    dve.tensor_tensor_reduce(z[:, q, P:3 * P], b[:, P:3 * P], tabs[:, s % H, :], 1.0, 3e38,
                                             ALU.add, ALU.min, zmin[:, q, 1:2]).then_inc(z_done, 1)
                if 1 <= s and s - 1 < NSLOT:
                    scale_p(s - 1)
                for name in jobs_of_slot.get(s, []):
                    j = job_at[name]
                    b = job_bank(name)
                    read = bank_read[j % 2]
                    if name == "kcvc":
                        dve.wait_ge(job_done, j + 1)
                        for i in range(2):
                            for lp in range(2):
                                for g in range(G):
                                    src = ps[g * HD:(g + 1) * HD, PJ[j % 2], i * S:(i + 1) * S]
                                    t = dve.tensor_tensor(
                                        R[i][lp * HD:(lp + 1) * HD, g, :, :], cmp_tokens(src, lp),
                                        peT[i][lp * HD:(lp + 1) * HD, :].unsqueeze(2).broadcast_to([HD, LP, NC]),
                                        ALU.add)
                                t.then_inc(r_ready, 1)
                        dve.wait_ge(r_ready, 4)
                        dve.engine_nop().then_inc(read, 1)
                    if name == "cm1":
                        k = slice(0, HD)
                        link(dve.memset(hx[k, 0:62], 0.0))
                        dve.wait_ge(job_done, j + 1)
                        dve.tensor_copy(hx[k, 0:30], b[k, 0:30])
                        dve.tensor_copy(hx[k, 32:62], b[k, 32:62]).then_inc(read, 1)
                        wait_job_read(dve, "cm1")
                        link(dve.tensor_tensor(hsq[k, 0:62], hx[k, 0:62], hx[k, 0:62], ALU.mult))
                        link(dve.tensor_scalar(hsq[k, 0:62], hsq[k, 0:62], 0.044715, 1.0, ALU.mult, ALU.add))
                        dve.tensor_tensor(ht[k, 0:62], hsq[k, 0:62], hx[k, 0:62], ALU.mult).then_inc(gelu_t, 1)
                    if name == "nq1":
                        dve.wait_ge(gelu_exp, 1)
                        k = slice(0, HD)
                        link(dve.tensor_scalar(hsq[k, 0:62], hsq[k, 0:62], 1.0, None, ALU.add))
                        link(dve.reciprocal(hsq[k, 0:62], hsq[k, 0:62]))
                        dve.tensor_tensor(hTk[k, 0:30], hsq[k, 0:30], hx[k, 0:30], ALU.mult).then_inc(gelu_done, 1)
                        dve.wait_ge(const_ready, 7)
                        for g in range(G):
                            o = 32 + NC * g
                            t = dve.tensor_tensor(hTv[k, g, :, 0:NC],
                                                  hsq[k, o:o + NC].unsqueeze(1).broadcast_to([HD, 4, NC]),
                                                  hx[k, o:o + NC].unsqueeze(1).broadcast_to([HD, 4, NC]), ALU.mult)
                        t.then_inc(gelu_done, 1)
                    if name == "cs":
                        dve.wait_ge(job_done, j + 1)
                        dve.wait_ge(ctab_ready, H)
                        dve.wait_ge(const_ready, 7)
                        cv = cz[:, :, :, 0:NC]
                        bv = b[:, 0:256].rearrange("p (n h g c) -> p n h g c", n=2, h=HG, g=G)
                        for g in range(G):
                            hs = slice(HG * g, HG * g + HG)
                            t = dve.tensor_tensor(cz[:, :, hs, 0:NC], bv[:, :, :, g, 0:NC], ctab[:, :, hs, 0:NC],
                                                  ALU.add)
                        t.then_inc(read, 1)
                        wait_job_read(dve, "cs")
                        link(dve.tensor_reduce(cmin, cv, AX.X, ALU.min))
                        dve.tensor_tensor(cv, cv, cmin.unsqueeze(3).broadcast_to([P, 2, H, NC]), ALU.subtract)\
                           .then_inc(cz_ready, 1)
                    if name[:2] == "om":
                        dve.wait_ge(job_done, j + 1)
                        add(int(name[2]), int(name[3]), PJ[j % 2]).then_inc(read, 1)
                if s == H - 1:
                    wait_job_read(dve, "kwvw", "vw1")
                    link(dve.tensor_scalar(gtmp, gtmp, 1.0, None, ALU.add))
                    link(dve.reciprocal(gates, gtmp))
                if s == CZ_SLOT:
                    dve.wait_ge(cexp_done, 1)
                    cv = cz[:, :, :, 0:NC]
                    link(dve.tensor_tensor(cv, cv, cmask[:, :, 0:NC].unsqueeze(2).broadcast_to([P, 2, H, NC]),
                                           ALU.mult))
                    link(dve.tensor_reduce(csum, cv, AX.X, ALU.add))
                    link(dve.tensor_scalar(csum, csum, 1e-30, None, ALU.max))
                    link(dve.reciprocal(crec, csum))
                    link(dve.tensor_tensor(crec, crec, gates.rearrange("p n (h b) -> p n h b", b=3)[:, :, :, 0],
                                           ALU.mult))
                    dve.tensor_tensor(cv, cv, crec.unsqueeze(3).broadcast_to([P, 2, H, NC]), ALU.mult)\
                       .then_inc(cp_ready, 1)
                if s == H - 1 + PV_LAG:
                    dve.wait_ge(pv_done, H)
                    dve.tensor_copy(xs[:, :, 0:512], ps[:, OB[0]:OB[1] + 1, :]).then_inc(o_read, 1)
            for n in range(NT):
                dve.wait_ge(pv_done, NSLOT + 1 + n)
                dve.tensor_copy(xs[:, n, 512:1024], ps[:, OB[n], :]).then_inc(o_read, 1)

            for n in range(NT):
                dve.wait_ge(half_done, n + 1)
                add(n, 0, 2 + 2 * n).then_inc(half_added, 1)
                dve.wait_ge(proj_done, n + 1)
                add(n, 1, 3 + 2 * n).then_inc(half_added, 1)
                dve.wait_ge(half_added, 2 * n + 2)
                square(n, 2 + n)
                scale(n, 2 + n)
                for half in range(2):
                    read_xT(2 * n + half, 6, gfT)

            dve.wait_ge(logits_done, 1)
            dve.wait_ge(router_in, 32)
            dve.wait_ge(iotas_ready, IOTAS)
            link(dve.tensor_tensor(lg, ps[:, OUT[1][0], 0:2 * E].rearrange("p (n e) -> p n e", n=2),
                                   br[:, :].unsqueeze(1).broadcast_to([P, 2, E]), ALU.add))
            dve.max(top[:, 0, :], lg[:, 0, :])
            link(dve.max(top[:, 1, :], lg[:, 1, :]))
            dve.max_index(topi[:, 0, :], top[:, 0, :], lg[:, 0, :])
            link(dve.max_index(topi[:, 1, :], top[:, 1, :], lg[:, 1, :]))
            link(dve.tensor_copy(topf, topi[:, :, 0:TOPK]))
            hot_v = hot.rearrange("p n k e -> p (n k) e")
            link(dve.tensor_tensor(hot_v, iota_e.unsqueeze(1).broadcast_to([P, 2 * TOPK, E]),
                                   topf.rearrange("p n k -> p (n k)").unsqueeze(2).broadcast_to([P, 2 * TOPK, E]),
                                   ALU.is_equal))
            dve.tensor_reduce(M, hot.rearrange("p n k e -> p n e k"), AX.X, ALU.add).then_inc(m_ready, 1)
            dve.tensor_tensor(tdiff, top[:, :, 0:TOPK], top[:, :, 0:1].broadcast_to([P, 2, TOPK]), ALU.subtract)\
               .then_inc(td_ready, 1)
            dve.wait_ge(m_ready, 1)
            dve.wait_ge(pos_done, 1)
            b = ps[:, OUT[1][1], :]
            link(dve.scalar_tensor_tensor(out=posp[:, :, 0:E], in0=b[:, 0:2 * E].rearrange("p (n e) -> p n e", n=2),
                                          scalar=1.0, in1=M, op0=ALU.add, op1=ALU.mult))

            def pick(b, place):
                for n in range(NT):
                    t = dve.tensor_scalar(pm[:, n, :], iota_t[:, 0:TOK], place(n), None, ALU.is_equal)
                t.then_inc(pm_ready, 1)

            def weigh(b, e, place):
                for n in range(NT):
                    t = dve.tensor_scalar(pw[:, n, :], iota_t, place(n), Wt[:, n, ds(e, 1)], ALU.is_equal, ALU.mult)
                t.then_inc(pw_ready, 1)

            def listed(e):
                return lambda n: posp[:, n, ds(e, 1)]

            def read_xgT(b):
                dve.wait_ge(xgT_done, b + 1)
                dve.tensor_tensor(xgT.rearrange("p (h j) t -> p j h t", h=2),
                                  ps[:, XTB, :].rearrange("p (j h t) -> p j h t", j=4, h=2),
                                  gfT.rearrange("p (h j) -> p j h", h=2).unsqueeze(3).broadcast_to([P, 4, 2, 64]),
                                  ALU.mult).then_inc(xgT_read, 1)

            def swiglu(b, between=None):
                dve.wait_ge(up_used, b * UP_UNITS + UP_UNITS)
                dve.tensor_scalar(t1, UP[:, :, 0:512:2], 7.0, None, ALU.min).then_inc(swi, 1)
                dve.tensor_scalar(t3, UP[:, :, 1:512:2], 7.0, -7.0, ALU.min, ALU.max).then_inc(swi, 1)
                dve.wait_ge(swi, b * 3 + 2)
                dve.scalar_tensor_tensor(out=t3, in0=t3, scalar=1.0, in1=t1, op0=ALU.add, op1=ALU.mult)\
                   .then_inc(swi, 1)
                dve.wait_ge(swi, b * 3 + 3)
                dve.wait_ge(sig_done, b + 1)
                dve.tensor_tensor(av, t3, t2, ALU.mult).then_inc(a_ready, 1)

            def read_aT(b):
                dve.wait_ge(aT_done, b + 1)
                dve.tensor_copy(aT[:, 2:4, :], UP[:, 1, 0:256].rearrange("p (a q) -> p a q", a=2))\
                   .then_inc(aT_read, 1)

            pick(0, listed(0))
            read_xgT(0)
            dve.wait_ge(te_ready, 1)
            link(dve.tensor_reduce(tsum, texp, AX.X, ALU.add))
            link(dve.reciprocal(trec, tsum))
            link(dve.tensor_tensor(tw, texp, trec.unsqueeze(2).broadcast_to([P, 2, TOPK]), ALU.mult))
            link(dve.tensor_tensor(hotw.rearrange("p n k e -> p (n k) e"), hot_v,
                                   tw.rearrange("p n k -> p (n k)").unsqueeze(2).broadcast_to([P, 2 * TOPK, E]),
                                   ALU.mult))
            dve.tensor_reduce(Wt[:, :, 0:E], hotw.rearrange("p n k e -> p n e k"), AX.X, ALU.add)\
               .then_inc(w_ready, 1)
            dve.wait_ge(xg_done, 1)
            pick(1, listed(1))
            dve.wait_ge(w_ready, 1)
            weigh(0, 0, listed(0))
            dve.wait_ge(cnt_done, 1)
            link(dve.tensor_copy(cnt[0:E], b[0:E, 64:65]))
            link(dve.tensor_tensor(flag[0:E], cnt[0:E].broadcast_to([E, MORE]), more_k[0:E], ALU.is_gt))
            dve.tensor_reduce(nflag[0:E], flag[0:E], AX.X, ALU.add).then_inc(nflag_ready, 1)
            swiglu(0)
            read_xgT(1)
            read_aT(0)
            dve.wait_ge(cT_done, 1)
            weigh(1, 1, listed(1))
            dve.wait_ge(xg_done, 2)
            pick(2, listed(2))
            dve.wait_ge(rank_done, 1)
            link(dve.tensor_copy(cnt[0:E], ps[0:E, OUT[0][0], 0:1]))
            link(dve.tensor_scalar(rank[0:E], more_k[0:E], 1.0 / CAP, -1.0, ALU.mult, ALU.add))
            link(dve.tensor_scalar(rank[0:E], rank[0:E], cnt[0:E], None, ALU.add))
            link(dve.tensor_tensor(Rsel[0:E], iota_o[0:E].unsqueeze(1).broadcast_to([E, MORE, NOV]),
                                   rank[0:E].unsqueeze(2).broadcast_to([E, MORE, NOV]), ALU.is_equal))
            link(dve.tensor_tensor(Rsel[0:E], Rsel[0:E], flag[0:E].unsqueeze(2).broadcast_to([E, MORE, NOV]),
                                   ALU.mult))
            link(dve.tensor_reduce(Rk[0:E], Rsel[0:E].rearrange("p k i -> p i k"), AX.X, ALU.add))
            dve.tensor_scalar(Re[0:E], Rk[0:E], ecol[0:E], None, ALU.mult).then_inc(rsel_ready, 1)
            link(dve.tensor_tensor(Rsel[0:E], Rsel[0:E], more_k[0:E].unsqueeze(2).broadcast_to([E, MORE, NOV]),
                                   ALU.mult))
            dve.tensor_reduce(Rb[0:E], Rsel[0:E].rearrange("p k i -> p i k"), AX.X, ALU.add)\
               .then_inc(rsel_ready, 2)
            dve.wait_ge(ovt_done, 1)
            link(dve.tensor_copy(ovt, ps[:, OUT[0][0], 64:65 + 2 * NOV]))
            dve.tensor_copy(ovi, ovt).then_inc(ovi_ready, 1)

            swiglu(1)
            read_xgT(2)
            read_aT(1)
            with dve.Fori(2, E - 1) as i:
                dve.wait_ge(cT_done, i)
                weigh(i, i, listed(i))
                dve.wait_ge(xg_done, i + 1)
                pick(i + 1, listed(i + 1))
                swiglu(i)
                read_xgT(i + 1)
                read_aT(i)
            dve.wait_ge(cT_done, E - 1)
            weigh(E - 1, E - 1, listed(E - 1))
            swiglu(E - 1)
            read_aT(E - 1)
            more = dve.value_load(ovi[0:1, 2 * NOV:2 * NOV + 1], min_val=0, max_val=NOV)
            with dve.If(more > 0):
                with dve.Fori(0, more) as o:
                    e = dve.value_load(ovi[0:1, ds(o, 1)], min_val=0, max_val=E - 1)
                    dve.wait_ge(xg_done, o + E)
                    dve.wait_ge(cT_done, o + E)
                    dve.wait_ge(pw_ready, o + E)
                    dve.tensor_scalar(pcol, posp[:, :, ds(e, 1)].rearrange("p n o -> p (n o)"),
                                      ovt[:, ds(o + NOV, 1)], None, ALU.subtract).then_inc(pcol_ready, 1)
                    dve.wait_ge(pcol_ready, o + 1)
                    pick(o + E, lambda n: pcol[:, n:n + 1])
                    weigh(o + E, e, lambda n: pcol[:, n:n + 1])
                    read_xgT(o + E)
                    swiglu(o + E)
                    read_aT(o + E)
                    dve.wait_ge(comb_done, o + E + 1)

            for n in range(NT):
                for half in range(2):
                    if n == 0:
                        dve.wait_ge(half_summed, half + 1)
                    else:
                        dve.wait_ge(comb_done, E)
                    add(n, half, OUT[n][half]).then_inc(half_added, 1)
                dve.wait_ge(half_added, 4 + 2 * n + 2)
                square(n, 4 + n)
                if n == 0:
                    dve.wait_ge(gfin_ready, 1)
                scale(n, 4 + n)
                for half in range(2):
                    h = slice(512 * half, 512 * half + 512)
                    dve.scalar_tensor_tensor(out=xs[:, n, h], in0=xt[:, n, h], scalar=rstd[:, 4 + n:5 + n],
                                             in1=gfin[:, h], op0=ALU.mult, op1=ALU.mult).then_inc(fin_ready, 1)


_INS = ['x', 'attn_norm_g', 'w_in', 'cmp_pe_k', 'cmp_pe_v', 'cmp_w1_k', 'cmp_w2_k', 'cmp_w1_v', 'cmp_w2_v', 'w_out',
        'ffn_norm_g', 'w_router', 'b_router', 'w_up', 'b_up', 'w_down', 'b_down', 'final_norm_g']


def kernel(**inputs):
    import numpy as _np
    import concourse.bacc as _bacc
    from concourse import mybir as _mybir
    from concourse.bass_utils import run_bass_kernel_spmd as _run

    nc = _bacc.Bacc("TRN2", target_bir_lowering=False, num_devices=1)
    arrays, args = {}, []
    for name in _INS:
        a = _np.ascontiguousarray(inputs[name])
        arrays[f"in_{name}_dram"] = a
        args.append(nc.dram_tensor(f"in_{name}_dram", a.shape, _mybir.dt.from_np(a.dtype), kind="ExternalInput").ap())
    shape = arrays["in_x_dram"].shape
    args.append(nc.dram_tensor("out_0_dram", shape, _mybir.dt.float32, kind="ExternalOutput").ap())
    hybrid_layer(nc, *args)
    r = _run(nc, [arrays], core_ids=[0])
    return r.results[0]["out_0_dram"]
```
